# Optimizing a Trainium2 kernel written in Bass

```python
import math
import jax, jax.numpy as jnp
from jax import lax
import numpy as np

D_MODEL = 1024
BATCH = 1
SEQ = 512
DEPTH = 1

CHUNK = 64
CONV_CH = 512
CONV_WIDTH = 31
N_HEADS = 8
HEAD_DIM = 64
N_KV = 2
ATTN_W = N_HEADS * HEAD_DIM
IDX_HEADS = 8
IDX_DIM = 32
TOPK_MAX = 256
Q_BLOCK = 128
REL_BUCKETS = 32
REL_MAX_DIST = 128
N_GROUPS = 4
EXPERTS_PER_GROUP = 8
N_EXPERTS = N_GROUPS * EXPERTS_PER_GROUP
EXPERT_FF = 256
TOP_IN_GROUP = 2
EPS = 1e-6

SPLITS = (2 * CONV_CH, ATTN_W, N_KV * HEAD_DIM, N_KV * HEAD_DIM,
          IDX_HEADS * IDX_DIM, IDX_DIM, IDX_HEADS, D_MODEL, D_MODEL)
IN_COLS = 2 * CONV_CH + ATTN_W + 2 * N_KV * HEAD_DIM + IDX_HEADS * IDX_DIM + IDX_DIM + IDX_HEADS + 2 * D_MODEL

kernel_name = "hybrid_conv_dsa_hmoe_block"

def rms_norm(x, g):
    xf = x.astype(jnp.float32)
    y = xf * lax.rsqrt(jnp.mean(xf * xf, axis=-1, keepdims=True) + EPS)
    return (y * g.astype(jnp.float32)).astype(x.dtype)

def layer_norm(x, g, b):
    xf = x.astype(jnp.float32)
    mu = jnp.mean(xf, axis=-1, keepdims=True)
    var = jnp.mean(jnp.square(xf - mu), axis=-1, keepdims=True)
    y = (xf - mu) * lax.rsqrt(var + EPS) * g.astype(jnp.float32) + b.astype(jnp.float32)
    return y.astype(x.dtype)

def rel_bucket(rel):
    nb = REL_BUCKETS // 2
    max_exact = nb // 2
    ret = jnp.where(rel < 0, nb, 0)
    n = jnp.abs(rel)
    nf = jnp.maximum(n, 1).astype(jnp.float32)
    large = max_exact + (jnp.log(nf / max_exact) / math.log(REL_MAX_DIST / max_exact)
                         * (nb - max_exact)).astype(jnp.int32)
    large = jnp.minimum(large, nb - 1)
    return ret + jnp.where(n < max_exact, n, large)

def conv_branch(u, conv_w, conv_b, ln_g, ln_b, w_o):
    a, gate = jnp.split(u, 2, axis=-1)
    v = a * jax.nn.sigmoid(gate)
    v = lax.conv_general_dilated(
        v, conv_w[:, None, :], window_strides=(1,),
        padding=[(CONV_WIDTH - 1, 0)],
        dimension_numbers=('NWC', 'WIO', 'NWC'),
        feature_group_count=CONV_CH) + conv_b
    v = jax.nn.silu(layer_norm(v, ln_g, ln_b))
    return v @ w_o

def sparse_attention(q, k, v, qi, ki, wi, rel_bias):
    B, L = q.shape[0], q.shape[1]
    topk = min(TOPK_MAX, L // 4)
    nblk = L // Q_BLOCK
    R = N_HEADS // N_KV
    key_pos = jnp.arange(L)
    gather = jax.vmap(lambda a, i: a[i])

    def to_blocks(a):
        return jnp.moveaxis(a.reshape((B, nblk, Q_BLOCK) + a.shape[2:]), 1, 0)

    def block(args):
        blk, qb, qib, wib = args
        t = blk * Q_BLOCK + jnp.arange(Q_BLOCK)
        dots = jnp.einsum('bqhd,bsd->bqhs', qib, ki).astype(jnp.float32) * (IDX_DIM ** -0.5)
        score = jnp.einsum('bqhs,bqh->bqs', jax.nn.relu(dots),
                           wib.astype(jnp.float32)) * (IDX_HEADS ** -0.5)
        limit = (t // CHUNK + 1) * CHUNK
        adm = key_pos[None, :] < limit[:, None]
        score = jnp.where(adm[None], score, -jnp.inf)
        vals, idx = lax.top_k(score, topk)
        valid = jnp.isfinite(vals)
        k_sel = gather(k, idx)
        v_sel = gather(v, idx)
        bias = rel_bias[rel_bucket(t[None, :, None] - idx)]
        bias = jnp.moveaxis(bias.reshape(B, Q_BLOCK, topk, N_KV, R), 2, -1)
        qg = qb.reshape(B, Q_BLOCK, N_KV, R, HEAD_DIM)
        logits = (jnp.einsum('bqgrd,bqkgd->bqgrk', qg, k_sel).astype(jnp.float32)
                  * (HEAD_DIM ** -0.5) + bias.astype(jnp.float32))
        logits = jnp.where(valid[:, :, None, None, :], logits, -jnp.inf)
        p = jax.nn.softmax(logits, axis=-1).astype(v.dtype)
        o = jnp.einsum('bqgrk,bqkgd->bqgrd', p, v_sel)
        return o.reshape(B, Q_BLOCK, ATTN_W)

    out = lax.map(block, (jnp.arange(nblk), to_blocks(q), to_blocks(qi), to_blocks(wi)))
    return jnp.moveaxis(out, 0, 1).reshape(B, L, ATTN_W)

def mixer(h, w_in, conv_w, conv_b, ln_g, ln_b, w_conv_out, w_attn_out, w_out, rel_bias):
    B, L, _ = h.shape
    proj = h @ w_in
    offs = [int(o) for o in np.cumsum(SPLITS)[:-1]]
    u_conv, q, k, v, qi, ki, wi, gc, ga = jnp.split(proj, offs, axis=-1)
    y_conv = conv_branch(u_conv, conv_w, conv_b, ln_g, ln_b, w_conv_out)
    y_attn = sparse_attention(
        q.reshape(B, L, N_HEADS, HEAD_DIM), k.reshape(B, L, N_KV, HEAD_DIM),
        v.reshape(B, L, N_KV, HEAD_DIM), qi.reshape(B, L, IDX_HEADS, IDX_DIM),
        ki, wi, rel_bias) @ w_attn_out
    merged = jax.nn.sigmoid(gc) * y_conv + jax.nn.sigmoid(ga) * y_attn
    return merged @ w_out

def hier_moe(h, w_gr, b_gr, w_er, b_er, w_gate, w_up, w_down):
    B, L, D = h.shape
    ht = h.reshape(-1, D)
    g_logits = (ht @ w_gr + b_gr).astype(jnp.float32)
    g_prob = jax.nn.softmax(g_logits, axis=-1)
    grp = jnp.argmax(g_logits, axis=-1)
    p_grp = jnp.take_along_axis(g_prob, grp[:, None], axis=-1)
    e_logits = (jnp.einsum('td,gde->tge', ht, w_er) + b_er).astype(jnp.float32)
    e_logits = jnp.take_along_axis(e_logits, grp[:, None, None], axis=1)[:, 0]
    top_vals, top_idx = lax.top_k(e_logits, TOP_IN_GROUP)
    p_in = jax.nn.softmax(top_vals, axis=-1) * p_grp
    in_w = jnp.einsum('tj,tje->te', p_in,
                      jax.nn.one_hot(top_idx, EXPERTS_PER_GROUP, dtype=jnp.float32))
    comb = jax.nn.one_hot(grp, N_GROUPS, dtype=jnp.float32)[:, :, None] * in_w[:, None, :]
    comb = jnp.moveaxis(comb, 1, 0).astype(h.dtype)

    def group_ffn(args):
        wg, wu, wd, c = args
        a = jnp.einsum('td,edf->tef', ht, wg)
        b = jnp.einsum('td,edf->tef', ht, wu)
        return jnp.einsum('tef,efd->td', jax.nn.silu(a) * b * c[:, :, None], wd)

    shp_in = (N_GROUPS, EXPERTS_PER_GROUP, D, EXPERT_FF)
    shp_out = (N_GROUPS, EXPERTS_PER_GROUP, EXPERT_FF, D)
    out = lax.map(group_ffn, (w_gate.reshape(shp_in), w_up.reshape(shp_in),
                              w_down.reshape(shp_out), comb)).sum(axis=0)
    return out.reshape(B, L, D)

def setup_inputs(seed: int = 0) -> dict:
    key = jax.random.key(seed)
    ks = jax.random.split(key, 24)
    nrm = lambda k, shape, scale: jax.random.normal(k, shape, jnp.float32) * scale
    D = D_MODEL
    return {
        "x": nrm(ks[0], (BATCH, SEQ, D), 1.0),
        "g_mix": 1.0 + nrm(ks[1], (DEPTH, D), 0.01),
        "w_in": nrm(ks[2], (DEPTH, D, IN_COLS), D ** -0.5),
        "conv_w": nrm(ks[3], (DEPTH, CONV_WIDTH, CONV_CH), CONV_WIDTH ** -0.5),
        "conv_b": nrm(ks[4], (DEPTH, CONV_CH), 0.01),
        "conv_ln_g": 1.0 + nrm(ks[5], (DEPTH, CONV_CH), 0.01),
        "conv_ln_b": nrm(ks[6], (DEPTH, CONV_CH), 0.01),
        "w_conv_out": nrm(ks[7], (DEPTH, CONV_CH, D), CONV_CH ** -0.5),
        "w_attn_out": nrm(ks[8], (DEPTH, ATTN_W, D), ATTN_W ** -0.5),
        "w_out": nrm(ks[9], (DEPTH, D, D), D ** -0.5),
        "rel_bias": nrm(ks[10], (REL_BUCKETS, N_HEADS), 0.5),
        "g_ffn": 1.0 + nrm(ks[11], (DEPTH, D), 0.01),
        "w_group_router": nrm(ks[12], (DEPTH, D, N_GROUPS), D ** -0.5),
        "b_group_router": nrm(ks[13], (DEPTH, N_GROUPS), 0.01),
        "w_expert_router": nrm(ks[14], (DEPTH, N_GROUPS, D, EXPERTS_PER_GROUP), D ** -0.5),
        "b_expert_router": nrm(ks[15], (DEPTH, N_GROUPS, EXPERTS_PER_GROUP), 0.01),
        "w_e_gate": nrm(ks[16], (DEPTH, N_EXPERTS, D, EXPERT_FF), D ** -0.5),
        "w_e_up": nrm(ks[17], (DEPTH, N_EXPERTS, D, EXPERT_FF), D ** -0.5),
        "w_e_down": nrm(ks[18], (DEPTH, N_EXPERTS, EXPERT_FF, D), EXPERT_FF ** -0.5),
        "g_final": 1.0 + nrm(ks[19], (D,), 0.01),
    }

def reference(x, g_mix, w_in, conv_w, conv_b, conv_ln_g, conv_ln_b, w_conv_out, w_attn_out,
              w_out, rel_bias, g_ffn, w_group_router, b_group_router, w_expert_router,
              b_expert_router, w_e_gate, w_e_up, w_e_down, g_final):
    for l in range(DEPTH):
        h = rms_norm(x, g_mix[l])
        x = x + mixer(h, w_in[l], conv_w[l], conv_b[l], conv_ln_g[l], conv_ln_b[l],
                      w_conv_out[l], w_attn_out[l], w_out[l], rel_bias)
        h = rms_norm(x, g_ffn[l])
        x = x + hier_moe(h, w_group_router[l], b_group_router[l], w_expert_router[l],
                         b_expert_router[l], w_e_gate[l], w_e_up[l], w_e_down[l])
    return rms_norm(x, g_final)


_drawn_inputs = setup_inputs


def setup_inputs(seed=0):
    import zlib

    import numpy as np

    out = dict(_drawn_inputs(seed))
    spreads = {}
    factors = {'conv_ln_g': 16.42,
     'conv_ln_b': 15.753,
     'b_group_router': 23.119,
     'b_expert_router': 15.564,
     'g_final': 32.144,
     'g_mix': 3.13,
     'conv_b': 2.685,
     'g_ffn': 5.189}
    for name, (base, spread) in spreads.items():
        noise = np.random.default_rng([zlib.crc32(name.encode()), seed]).standard_normal(out[name].shape)
        drawn = base * np.exp(spread * noise) if base else spread * noise
        out[name] = __import__('jax').numpy.asarray(drawn.astype(out[name].dtype))
    for name, factor in factors.items():
        out[name] = (out[name] * factor).astype(out[name].dtype)
    return out
```

```python
from contextlib import ExitStack

import numpy as np

import concourse.bass as bass
from concourse import mybir

F32 = mybir.dt.float32
BF16 = mybir.dt.bfloat16
I32 = mybir.dt.int32
U32 = mybir.dt.uint32
ALU = mybir.AluOpType
ACT = mybir.ActivationFunctionType
AX = mybir.AxisListType.X

P = 128
BANK = 512
NEG = -3.0e38
MASKED = -1.0e30
EPS = 1e-6
CHUNK = 64
HEAD_DIM = 64
TOPK = 128
BIG_ROW = 4096

BUCKET_STARTS = [0, 1, 2, 3, 4, 5, 6, 7, 8, 12, 16, 23, 32, 46, 64, 91]


def bucket_runs(lowest, highest):
    ends = [s - 1 for s in BUCKET_STARTS[1:]] + [1 << 20]
    runs = []
    for k in range(15, -1, -1):
        runs.append((-ends[k], -max(BUCKET_STARTS[k], 1), 16 + k))
    for k in range(16):
        runs.append((BUCKET_STARTS[k], ends[k], k))
    clipped = [(max(a, lowest), min(b, highest), k) for a, b, k in runs]
    return [(a, b, k) for a, b, k in clipped if a <= b]


def spread(ap, axis, n):
    shape = list(ap.shape)
    shape.insert(axis, n)
    return ap.unsqueeze(axis).to_broadcast(shape)


def build(nc, x, g_mix, w_in, conv_w, conv_b, conv_ln_g, conv_ln_b, w_conv_out, w_attn_out, w_out,
          rel_bias, g_ffn, w_gr, b_gr, w_er, b_er, w_e_gate, w_e_up, w_e_down, g_final, out):
    _, T, D = x.shape
    TB = T // P
    KD = D // P
    C = conv_w.shape[2]
    CC = C // P
    TAPS = conv_w.shape[1]
    PAD = TAPS - 1
    H = rel_bias.shape[1]
    NG, EG = w_er.shape[1], w_er.shape[3]
    NE = NG * EG
    FF = w_e_gate.shape[3]
    SLOTS = 64
    PAIRS = NE // 2
    RING = 4
    MAXT = 32
    assert PAIRS + (2 * T - PAIRS) // SLOTS < MAXT
    IH, ID = 8, 32
    LW = NG + NE
    GROUP = 4
    QI0 = 2 * C + H * HEAD_DIM + 2 * P
    KI0 = QI0 + IH * ID
    GATE0 = KI0 + ID + IH
    NSMALL = ID + IH

    h2_dram = nc.dram_tensor("h2_rows", (T, D), F32).ap()
    y_dram = nc.dram_tensor("expert_rows", (2 * T, D), F32).ap()
    bias_dram = nc.dram_tensor("bias_by_distance", (H, P, 640), F32).ap()

    with ExitStack() as ctx:
        def sb(name, shape, dt=F32):
            return ctx.enter_context(nc.sbuf_tensor(name, shape, dt))

        def sem(name):
            return ctx.enter_context(nc.semaphore(name))

        bank = [ctx.enter_context(nc.psum_tensor(f"bank{i}", [P, BANK], F32)) for i in range(8)]

        REG = 2 * 3 * 2048
        region = [sb("region0", [P, REG]), sb("region1", [P, REG])]
        r0, r1 = region
        win = [r0[:, s * 4096:(s + 1) * 4096].rearrange("p (k n) -> p k n", k=KD) for s in range(2)]
        hT = r0[:, 8192:12288].rearrange("p (k n) -> p k n", k=KD)
        wco = r0[:, 0:4096].rearrange("p (k n) -> p k n", k=CC)
        wao = r0[:, 4096:8192].rearrange("p (k n) -> p k n", k=CC)
        hrow = r1[:, 0:4096].rearrange("p (b n) -> p b n", b=TB)
        relu_off = {}
        at = 0
        for b in range(1, TB):
            relu_off[b] = at
            at += IH * P * (b + 1)
        bias = r1[:, 0:4096].rearrange("p (h n) -> p h n", h=H)
        prob = [r1[:, 4096 + s * 2048:6144 + s * 2048].rearrange("p (r n) -> p r n", r=4) for s in range(2)]
        pT = r1[:, 8192:10240].rearrange("p (s r n) -> p s r n", s=TB, r=4)
        kT = r1[:, 10240:11264].rearrange("p (g n) -> p g n", g=2)
        bm = r1[:, 11264:12288].rearrange("p (u n) -> p u n", u=2)
        wout = r1[:, 0:8192].rearrange("p (k n) -> p k n", k=KD)

        w_gu = [r[:, 0:8192].rearrange("p (e m k f) -> p e m k f", e=2, m=2, k=KD) for r in region]
        w_dn = [r[:, 8192:12288].rearrange("p (e j n) -> p e j n", e=2, j=2) for r in region]

        xr = sb("x_rows", [P, TB, D])
        gates = sb("gates", [P, 2 * KD, T])
        gA, gB = gates[:, 0:KD, :], gates[:, KD:2 * KD, :]
        h2row = gates[:, KD:2 * KD, :].rearrange("p k n -> p (k n)").rearrange("p (b n) -> p b n", b=TB)
        gflat = gates[:, :, :].rearrange("p k n -> p (k n)")
        xg = gflat[:, 0:1024]
        xTs = gflat[:, 1024:2048].rearrange("p (k n) -> p k n", k=KD)
        hid = gflat[:, 2048:2304]
        sil = gflat[:, 2304:2560]
        hidT = gflat[:, 2560:2816].rearrange("p (j n) -> p j n", j=2)
        ring = gflat[:, 4096:8192].rearrange("p (u n) -> p u n", u=RING)
        yrow = ring
        conv_buf = sb("conv_buf", [P, 2 * CC, T])
        yv, sT = conv_buf[:, 0:CC, :], conv_buf[:, CC:2 * CC, :]
        h2T = conv_buf
        ys = conv_buf[:, 0:4, :].rearrange("p (u k) n -> p u (k n)", u=2)
        qT = sb("qT", [P, CC, T])
        g_bc = qT[:, :, :].rearrange("p k n -> p (k n)").rearrange("p (u n) -> p u n", u=2)
        qiT = sb("qiT", [P, 2, T])
        kiT = sb("kiT", [P, T])
        vrow = sb("v_rows", [P, TB, P])
        glu = sb("glu", [P, CC, PAD + T])
        oT = glu[:, :, 0:T]
        sig = sb("sig", [P, 2, T])
        score = sb("score", [P, T])
        work = sb("work", [P, T])
        vT, wiT = work, score[0:IH, :]
        mask = sb("mask", [P, 1280])
        MOFF = [0, 128, 384, 768]

        ident = sb("ident", [P, P])
        ones = sb("ones", [P, P])
        ones_b = sb("ones_b", [P, P], BF16)
        before = sb("before", [P, P], BF16)
        iota64 = sb("iota64", [P, 64])
        part1 = sb("part1", [P, 1])
        blkcode = sb("blkcode", [P, 2 * TB])
        half32 = sb("half32", [P, NE])
        rev = sb("rev", [P, EG])
        mhalf = sb("mhalf", [P, 1])
        cvrow = r1[0:TAPS + 3, 4096:4096 + C]
        cv = sb("cv", [P, CC, TAPS + 3])
        gmix = sb("gmix", [P, KD])
        relbT = sb("relbT", [H, 32])
        gdist = sb("gdist", [H, 640])
        wsm = r1[:, 11264:11264 + KD * NSMALL].rearrange("p (k n) -> p k n", k=KD)
        wi = sb("wi", [P, TB, IH])
        ss = sb("ss", [P, 3, TB])
        rs = sb("rs", [P, 3, TB])
        m8 = sb("m8", [P, 8])
        mx = sb("mx", [P, 2, 4])
        nm = sb("nm", [P, 2, 4])
        sm = sb("sm", [P, 2, 4])
        ri = sb("ri", [P, 2, 4])
        wr = sb("wr", [P, KD, LW])
        wr_g = sb("wr_g", [P, KD, NG])
        wr_e = sb("wr_e", [P, NG, KD, EG])
        br = sb("br", [P, LW])
        gluf = glu[:, :, :].rearrange("p c n -> p (c n)")
        cut = [0]

        def piece(words):
            cut[0] += words
            return gluf[:, cut[0] - words:cut[0]]

        lgT = sig[0:LW, 0, :]
        lg = piece(TB * LW).rearrange("p (b n) -> p b n", b=TB)
        gw = piece(12 * TB * EG).rearrange("p (u b n) -> p u b n", u=12, b=TB)
        gs = piece(16 * TB).rearrange("p (u b) -> p u b", u=16)
        e4 = piece(TB * NE).rearrange("p (b g e) -> p b g e", b=TB, g=NG)
        Mf = piece(2 * TB * NE).rearrange("p (c b e) -> p c b e", c=2, b=TB)
        Mb = mask[:, 768:832].bitcast(BF16).rearrange("p (b e) -> p b e", b=TB)
        Mpre = mask[:, 832:896].bitcast(BF16).rearrange("p (b e) -> p b e", b=TB)
        Mtot = mask[:, 896:912].bitcast(BF16)
        big = piece(2 * TB * NE).rearrange("p (c b e) -> p c b e", c=2, b=TB)
        posr = piece(TB * NE).rearrange("p (b e) -> p b e", b=TB)
        cnt = sb("cnt", [P, NE])
        cnti = sb("cnti", [P, NE], I32)
        nseg = sb("nseg", [P, PAIRS])
        tend = sb("tend", [P, PAIRS])
        hib = sb("hib", [P, NE])
        tab = sb("tab", [P, PAIRS + 1], I32)
        posc = sb("posc", [P, 2 * TB])
        hic = sb("hic", [P, 2 * TB])
        posi = sb("posi", [P, 2 * TB], I32)
        loi = sb("loi", [P, 2 * TB], I32)
        segi = sb("segi", [P, 2 * TB], I32)
        hi = sb("hi", [P, 2 * TB])
        ohhi = piece(2 * TB * 64).rearrange("p (c n) -> p c n", c=2 * TB)
        ohlo = mask[:, 0:256].bitcast(BF16).rearrange("p (c n) -> p c n", c=2 * TB)
        ohv = mask[:, 256:768].bitcast(BF16).rearrange("p (c u n) -> p c u n", c=2 * TB, u=2)
        inv = sb("inv", [P, MAXT])
        dst = sb("dst", [P, MAXT])
        dsti = sb("dsti", [P, MAXT], I32)
        toki = sb("toki", [P, MAXT], I32)
        sidx = sb("sidx", [P, MAXT], U32)
        gidx = sb("gidx", [P, MAXT + RING + 1], U32)
        carrier = sb("carrier", [P, 5])
        gi1 = sb("gi1", [P, RING], U32)
        si1 = sb("si1", [P, 2], U32)
        wts = sb("wts", [P, 2, TB])

        ld_x = [sem(f"ld_x{b}") for b in range(TB)]
        ld_rows = sem("ld_rows")
        ld_gmix = sem("ld_gmix")
        ld_relb = sem("ld_relb")
        ld_win = [sem("ld_win0"), sem("ld_win1")]
        ld_small = sem("ld_small")
        ld_wco = sem("ld_wco")
        ld_wao = sem("ld_wao")
        ld_wout = sem("ld_wout")
        ld_router = sem("ld_router")
        ld_gbc = sem("ld_gbc")
        st_bias = sem("st_bias")
        ld_bias = sem("ld_bias")
        st_h2 = sem("st_h2")
        ld_gu = [sem("ld_gu0"), sem("ld_gu1")]
        ld_dn = [sem("ld_dn0"), sem("ld_dn1")]
        gathered = [sem(f"gathered{u}") for u in range(RING)]
        scattered = [sem("scattered0"), sem("scattered1")]
        ld_y = [sem("ld_y0"), sem("ld_y1")]
        st_out = sem("st_out")
        names = """consts_ready ss_done var_ready rstd_ready h_ready cv_mm xt_mm xt_ev g_ready proj_mm proj_ev
            glu_done conv_step vt_mm vt_ev ix_mm ix_relu ix_acc mask_ready conv_ready ln_mm yc_ready sq_ready
            lnvar_ready lnstd_ready z_ready silu_ready co_mm co_ev bm_ready qk_mm lg_done nm_ready ex_done
            p_ready pt_mm pt_ev pv_mm ot_ev ao_mm ao_ev merged wo_mm wo_ev h2_ready x2_mm x2_ev wr_ready
            rt_mm rt_ev exp_in exp_out m_ready rank_mm oh_ready tab_mm tab_ready gu_mm silu_g hid_ready
            hidT_mm hidT_ev y_mm yev_a yev_v xg_mm xtev_a xtev_v idx_copy y_add o_ready dve_chain pool_chain
            ys_free xg_ready sidx_copy""".split()
        S = {n: sem(n) for n in names}

        block = ctx.enter_context(nc.Block())
        group_col = [g * GROUP * P for g in range(4)] + [GATE0 + g * GROUP * P for g in range(4)]
        attn = [(b, g) for b in range(TB) for g in range(2)]
        tiles_before = [sum(b2 + 1 for b2, _ in attn[:i]) for i in range(len(attn) + 1)]

        w_in2 = w_in[0].rearrange("(p k) n -> p k n", k=KD)

        @block.sync
        def _(sp):
            for b in range(TB):
                sp.dma_start(xr[:, b, :], x[0, b * P:(b + 1) * P, :]).then_inc(ld_x[b], 16)
            for g in range(8):
                if g >= 2:
                    sp.wait_ge(S["proj_mm"], GROUP * (g - 1) + (1 if g - 2 > 3 else 0))
                sp.dma_start(win[g % 2], w_in2[:, :, group_col[g]:group_col[g] + GROUP * P])\
                    .then_inc(ld_win[g % 2], 16)
            sp.wait_ge(S["proj_mm"], 29)
            sp.dma_start(wco, w_conv_out[0].rearrange("(k p) n -> p k n", p=P)).then_inc(ld_wco, 16)
            sp.wait_ge(S["proj_mm"], 33)
            sp.dma_start(wao, w_attn_out[0].rearrange("(k p) n -> p k n", p=P)).then_inc(ld_wao, 16)
            sp.wait_ge(S["g_ready"], 1)
            sp.dma_start(bias_dram, spread(gdist[:], 1, P)).then_inc(st_bias, 16)
            sp.wait_ge(st_bias, 16)
            sp.wait_ge(S["mask_ready"], TB - 1)
            sp.dma_start(bias, bass.AP(bias_dram.tensor, P - 1, [[640 - 1, P], [P * 640, H], [1, T]])).then_inc(ld_bias, 16)
            sp.wait_ge(S["qk_mm"], 4 * len(attn))
            sp.dma_start(g_bc[:, 0, :], g_ffn.to_broadcast([P, D])).then_inc(ld_gbc, 16)
            sp.dma_start(g_bc[:, 1, :], g_final.rearrange("(a n) -> a n", a=1).to_broadcast([P, D]))\
                .then_inc(ld_gbc, 16)
            sp.wait_ge(S["pv_mm"], len(attn))
            sp.dma_start(wout, w_out[0].rearrange("(k p) n -> p k n", p=P)).then_inc(ld_wout, 16)

            def load_pair(slot, pair):
                for e in range(2):
                    ex = pair * 2 + e
                    for m, w in enumerate((w_e_gate, w_e_up)):
                        sp.dma_start(w_gu[slot][:, e, m, :, :],
                                     w[0, bass.ds(ex, 1)].rearrange("a (p k) f -> p (a k) f", k=KD))\
                            .then_inc(ld_gu[slot], 16)

            def load_down(slot, pair):
                for e in range(2):
                    ex = pair * 2 + e
                    sp.dma_start(w_dn[slot][:, e, :, :],
                                 w_e_down[0, bass.ds(ex, 1)].rearrange("a (p j) n -> p (a j) n", j=2))\
                        .then_inc(ld_dn[slot], 16)

            sp.wait_ge(S["ao_mm"], KD)
            load_pair(0, 0)
            load_down(0, 0)
            sp.wait_ge(S["wo_mm"], 2 * TB)
            load_pair(1, 1)
            load_down(1, 1)
            for b in range(TB):
                sp.wait_ge(S["h2_ready"], b + 1)
                sp.dma_start(h2_dram[b * P:(b + 1) * P, :], h2row[:, b, :]).then_inc(st_h2, 16)
            sp.wait_ge(S["tab_ready"], 1)
            with sp.Fori(1, PAIRS // 2) as i:
                for slot in range(2):
                    used = sp.value_load(tab[0:1, bass.ds(2 * i - 1 + slot, 1)], min_val=1, max_val=MAXT)
                    sp.wait_ge(S["gu_mm"], used)
                    load_pair(slot, 2 * i + slot)
                    sp.wait_ge(S["y_mm"], 2 * used)
                    load_down(slot, 2 * i + slot)
            tiles = sp.value_load(tab[0:1, PAIRS:PAIRS + 1], min_val=PAIRS, max_val=MAXT - 1)
            for n in range(2):
                sp.wait_ge(scattered[n], ((tiles + (1 + n)) // 2) * 16)
            for b in range(TB):
                if b >= 2:
                    sp.wait_ge(S["y_add"], 2 * (b - 1))
                for c in range(2):
                    sp.dma_start(yrow[:, 2 * (b % 2) + c, :], y_dram[c * T + b * P:c * T + (b + 1) * P, :])\
                        .then_inc(ld_y[b % 2], 16)
            for b in range(TB):
                sp.wait_ge(S["o_ready"], b + 1)
                sp.dma_start(out[0, b * P:(b + 1) * P, :], xr[:, b, :]).then_inc(st_out, 16)
            sp.wait_ge(st_out, 16 * TB)

        @block.gpsimd
        def _(pool):
            g = nc.gpsimd
            done = [0]

            def link(ins):
                done[0] += 1
                ins.then_inc(S["pool_chain"], 1)
                pool.wait_ge(S["pool_chain"], done[0])

            for name in ("proj_ev", "hid_ready", "hidT_mm", "hidT_ev", "yev_a", "yev_v", "ys_free"):
                pool.sem_inc(S[name], 1)
            g.memset(mhalf[:], -0.5)
            link(g.memset(ident[:], 0.0))
            link(g.affine_select(out=ident[:], in_=ident[:], compare_op=ALU.not_equal, fill=1.0, base=0,
                                 pattern=[[-1, P]], channel_multiplier=1))
            g.memset(ones[:], 1.0)
            for c in range(CC):
                g.memset(glu[:, c, 0:PAD], 0.0)
            g.memset(gdist[:], 0.0)
            g.memset(ones_b[:], 1.0).then_inc(S["consts_ready"], 1)
            pool.wait_ge(S["consts_ready"], 1)
            for b in range(TB):
                pool.wait_ge(S["var_ready"], b + 1)
                g.tensor_tensor(rs[:, 0, b:b + 1], ss[:, 0, b:b + 1], mhalf[:], ALU.pow)\
                    .then_inc(S["rstd_ready"], 1)
            g.affine_select(out=before[:], in_=ones_b[:], compare_op=ALU.is_gt, fill=0.0, base=0,
                            pattern=[[1, P]], channel_multiplier=-1)
            g.iota(iota64[:], pattern=[[1, 64]], base=0, channel_multiplier=0, allow_small_or_imprecise_dtypes=True)
            g.iota(part1[:], pattern=[[1, 1]], base=1, channel_multiplier=1, allow_small_or_imprecise_dtypes=True)
            g.iota(blkcode[:], pattern=[[T, 2], [P, TB]], base=0, channel_multiplier=0,
                   allow_small_or_imprecise_dtypes=True)
            g.iota(half32[:], pattern=[[0, PAIRS], [32, 2]], base=0, channel_multiplier=0,
                   allow_small_or_imprecise_dtypes=True)
            g.iota(rev[:], pattern=[[-1, EG]], base=EG, channel_multiplier=0, allow_small_or_imprecise_dtypes=True)
            link(g.memset(mask[:, 0:P], 0.0))
            g.memset(mask[0:CHUNK, CHUNK:P], MASKED).then_inc(S["consts_ready"], 1)
            pool.wait_ge(ld_bias, 16)
            pool.wait_ge(S["consts_ready"], 2)
            for i, (b, gr) in enumerate(attn):
                n = P * (b + 1)
                if b and gr == 0:
                    pool.wait_ge(S["mask_ready"], b)
                for r in range(4):
                    at_ = 4 * i + r
                    if at_ >= 2:
                        pool.wait_ge(S["lg_done"], at_ - 1)
                    m0 = T - n
                    g.tensor_tensor(bm[:, at_ % 2, 0:n], bias[:, 4 * gr + r, m0:T], mask[:, MOFF[b]:MOFF[b] + n],
                                    ALU.add).then_inc(S["bm_ready"], 1)
            for b in range(TB):
                pool.wait_ge(S["var_ready"], TB + b + 1)
                g.tensor_tensor(rs[:, 1, b:b + 1], ss[:, 1, b:b + 1], mhalf[:], ALU.pow)\
                    .then_inc(S["rstd_ready"], 1)
            pool.wait_ge(st_h2, 16 * TB)
            pool.wait_ge(S["x2_mm"], 2 * TB)
            pool.wait_ge(S["tab_ready"], 2)

            def hold(n, free=None):
                ins = g.tensor_tensor(carrier[:, n:n + 1], mhalf[:], mhalf[:], ALU.add)
                if free is not None:
                    ins.then_inc(free, 1)

            last_token = pool.to_reg(T - 1)
            last_row = pool.to_reg(2 * T - 1)

            def gather(t, u):
                g.tensor_copy(gi1[:, u:u + 1], gidx[:, bass.ds(t, 1)] if not isinstance(t, int) else gidx[:, t:t + 1])\
                    .then_inc(S["idx_copy"], 1)
                pool.wait_ge(S["idx_copy"], t + 1)
                hold(0)
                g.indirect_dma_start(out=ring[:, u, :], out_offset=None, in_=h2_dram,
                                     in_offset=bass.IndirectOffsetOnAxis(ap=gi1[:, u:u + 1], axis=0),
                                     bounds_check=last_token, oob_is_err=False).then_inc(gathered[u], 16)

            pool.wait_ge(S["x2_ev"], 2 * TB)
            g.memset(si1[:, 1:2], BIG_ROW).then_inc(S["sidx_copy"], 1)
            pool.wait_ge(S["sidx_copy"], 1)
            g.indirect_dma_start(out=y_dram, out_offset=bass.IndirectOffsetOnAxis(ap=si1[:, 1:2], axis=0),
                                 in_=ys[:, 1, :], in_offset=None, bounds_check=last_row, oob_is_err=False)\
                .then_inc(scattered[1], 16)
            tiles = pool.value_load(tab[0:1, PAIRS:PAIRS + 1], min_val=PAIRS, max_val=MAXT - 1)
            for u in range(RING):
                gather(u, u)
            pool.wait_ge(gathered[0], 16)
            g.tensor_copy(xg, ring[:, 0, :]).then_inc(S["xg_ready"], 1)
            pool.wait_ge(S["xg_ready"], 1)
            gather(RING, 0)
            with pool.Fori(0, MAXT // RING) as i:
                for q in range(RING):
                    t = RING * i + q
                    u = (q + 1) % RING
                    with pool.If(t < tiles):
                        pool.wait_ge(gathered[u], 16 * i + (16 if u else 32))
                        pool.wait_ge(S["xg_mm"], 2 * t + 2)
                        hold(3)
                        g.tensor_copy(xg, ring[:, u, :]).then_inc(S["xg_ready"], 1)
                        pool.wait_ge(S["xg_ready"], t + 2)
                        hold(4)
                        gather(t + (RING + 1), u)
                        g.tensor_copy(si1[:, q % 2:q % 2 + 1], sidx[:, bass.ds(t, 1)]).then_inc(S["sidx_copy"], 1)
                        pool.wait_ge(S["sidx_copy"], t + 2)
                        pool.wait_ge(S["yev_a"], t + 2)
                        pool.wait_ge(S["yev_v"], t + 2)
                        hold(1)
                        g.indirect_dma_start(out=y_dram,
                                             out_offset=bass.IndirectOffsetOnAxis(ap=si1[:, q % 2:q % 2 + 1], axis=0),
                                             in_=ys[:, q % 2, :], in_offset=None,
                                             bounds_check=last_row, oob_is_err=False).then_inc(scattered[q % 2], 16)
                        pool.wait_ge(scattered[(q - 1) % 2], 32 * i + 16 * (q // 2 + 1))
                        hold(2, S["ys_free"])
            for b in range(TB):
                pool.wait_ge(S["var_ready"], 2 * TB + b + 1)
                g.tensor_tensor(rs[:, 2, b:b + 1], ss[:, 2, b:b + 1], mhalf[:], ALU.pow)\
                    .then_inc(S["rstd_ready"], 1)

        @block.tensor
        def _(pe):
            mm = nc.tensor.matmul
            tr = nc.tensor.transpose
            pe.wait_ge(S["consts_ready"], 1)
            pe.wait_ge(ld_rows, 64)
            for c in range(CC):
                last = tr(bank[0][:, c * (TAPS + 3):(c + 1) * (TAPS + 3)], cvrow[:, c * P:(c + 1) * P],
                          ident[0:TAPS + 3, 0:TAPS + 3])
            last.then_inc(S["cv_mm"], 1)

            def transpose_rows(rows, ready, mm_sem, ev_sem, n0):
                for b in range(TB):
                    pe.wait_ge(ready, n0 + b + 1)
                    view = rows[:, b, :].rearrange("p (q k) -> p k q", k=KD)
                    for kh in range(2):
                        n = 2 * b + kh
                        if n >= 2:
                            pe.wait_ge(ev_sem, n - 1)
                        for kk in range(4):
                            last = tr(bank[6 + n % 2][:, kk * P:(kk + 1) * P], view[:, 4 * kh + kk, :], ident[:])
                        last.then_inc(mm_sem, 1)

            transpose_rows(hrow, S["h_ready"], S["xt_mm"], S["xt_ev"], 0)
            pe.wait_ge(S["xt_ev"], 2 * TB)

            def project(j, parity, w):
                pe.wait_ge(S["proj_ev"], j + 1)
                m = w.shape[2]
                for k in range(KD):
                    last = mm(bank[parity][0:m, :], w[:, k, :], hT[:, k, :], start=(k == 0), stop=(k == KD - 1))
                last.then_inc(S["proj_mm"], 1)

            pe.wait_ge(S["proj_ev"], 2)
            with pe.Fori(0, 2) as i:
                for slot in range(2):
                    pe.wait_ge(ld_win[slot], 16 * i + 16)
                    for q in range(GROUP):
                        project(8 * i + (4 * slot + q), q % 2, win[slot][:, :, q * P:(q + 1) * P])
            pe.wait_ge(ld_small, 16)
            project(16, 0, wsm)
            pe.wait_ge(S["proj_ev"], 19)
            for b in range(TB):
                last = tr(bank[7][:, b * IH:(b + 1) * IH], wiT[:, b * P:(b + 1) * P], ident[0:IH, 0:IH])
            last.then_inc(S["vt_mm"], 1)
            for b in range(TB):
                last = tr(bank[6][:, b * P:(b + 1) * P], vT[:, b * P:(b + 1) * P], ident[:])
            last.then_inc(S["vt_mm"], 1)
            for b in range(1, TB):
                n = P * (b + 1)
                for hb in range(2):
                    turn = 2 * (b - 1) + hb
                    for i in range(4):
                        if turn:
                            pe.wait_ge(S["ix_relu"], 4 * (turn - 1) + i + 1)
                        mm(bank[2 + i][:, 0:n], qiT[32 * i:32 * i + 32, hb, b * P:(b + 1) * P],
                           kiT[32 * i:32 * i + 32, 0:n], start=True, stop=True).then_inc(S["ix_mm"], 1)
            with pe.Fori(0, 2) as i:
                for slot in range(2):
                    pe.wait_ge(ld_win[slot], 16 * i + 48)
                    for q in range(GROUP):
                        project(8 * i + (17 + 4 * slot + q), (q + 1) % 2, win[slot][:, :, q * P:(q + 1) * P])
            pe.wait_ge(S["conv_ready"], 1)
            pe.wait_ge(S["vt_ev"], 2)
            for c in range(CC):
                last = mm(bank[6][:], ones[:], yv[:, c, :], start=(c == 0), stop=(c == CC - 1))
            last.then_inc(S["ln_mm"], 1)
            for c in range(CC):
                pe.wait_ge(S["sq_ready"], c + 1)
                last = mm(bank[7][:], ones[:], sT[:, c, :], start=(c == 0), stop=(c == CC - 1))
            last.then_inc(S["ln_mm"], 1)
            pe.wait_ge(ld_wco, 16)
            pe.wait_ge(S["silu_ready"], CC)
            pe.wait_ge(S["proj_ev"], 35)
            for n in range(KD):
                if n >= 2:
                    pe.wait_ge(S["co_ev"], n - 1)
                for c in range(CC):
                    last = mm(bank[n % 2][:], wco[:, c, n * P:(n + 1) * P], sT[:, c, :],
                              start=(c == 0), stop=(c == CC - 1))
                last.then_inc(S["co_mm"], 1)

            def logits(i):
                b, gr = attn[i]
                n = P * (b + 1)
                for r in range(4):
                    h = 4 * gr + r
                    lo = HEAD_DIM * (h % 2)
                    if i:
                        pe.wait_ge(S["lg_done"], 4 * (i - 1) + r + 1)
                    mm(bank[2 + r][:, 0:n], qT[lo:lo + HEAD_DIM, h // 2, b * P:(b + 1) * P],
                       kT[lo:lo + HEAD_DIM, gr, 0:n], start=True, stop=True).then_inc(S["qk_mm"], 1)

            pe.wait_ge(S["ix_relu"], 24)
            logits(0)
            pe.wait_ge(S["co_ev"], KD)
            for i, (b, gr) in enumerate(attn):
                if i + 1 < len(attn):
                    logits(i + 1)
                pe.wait_ge(S["p_ready"], i + 1)
                for s in range(b + 1):
                    n = tiles_before[i] + s
                    if n >= 2:
                        pe.wait_ge(S["pt_ev"], n - 1)
                    for r in range(4):
                        last = tr(bank[6 + n % 2][:, r * P:(r + 1) * P], prob[i % 2][:, r, s * P:(s + 1) * P], ident[:])
                    last.then_inc(S["pt_mm"], 1)
                pe.wait_ge(S["pt_ev"], tiles_before[i + 1])
                if i >= 2:
                    pe.wait_ge(S["ot_ev"], i - 1)
                for s in range(b + 1):
                    for par in range(2):
                        lo = HEAD_DIM * par
                        last = mm(bank[i % 2][lo:lo + HEAD_DIM, 0:2 * P],
                                  vrow[:, s, gr * HEAD_DIM:(gr + 1) * HEAD_DIM], pT[:, s, par::2, :],
                                  start=(s == 0), stop=(s == b))
                last.then_inc(S["pv_mm"], 1)
            pe.wait_ge(ld_wao, 16)
            pe.wait_ge(S["ot_ev"], len(attn))
            for n in range(KD):
                if n >= 2:
                    pe.wait_ge(S["ao_ev"], n - 1)
                for c in range(CC):
                    last = mm(bank[n % 2][:], wao[:, c, n * P:(n + 1) * P], oT[:, c, :],
                              start=(c == 0), stop=(c == CC - 1))
                last.then_inc(S["ao_mm"], 1)
            pe.wait_ge(ld_wout, 16)
            for m in range(2 * TB):
                b, hf = m // 2, m % 2
                if m >= 4:
                    pe.wait_ge(S["wo_ev"], m - 3)
                for k in range(KD):
                    if m == 0:
                        pe.wait_ge(S["merged"], k + 1)
                    last = mm(bank[2 + m % 4][:], gA[:, k, b * P:(b + 1) * P], wout[:, k, hf * BANK:(hf + 1) * BANK],
                              start=(k == 0), stop=(k == KD - 1))
                last.then_inc(S["wo_mm"], 1)
            transpose_rows(h2row, S["h2_ready"], S["x2_mm"], S["x2_ev"], 0)
            pe.wait_ge(S["wr_ready"], 1)
            pe.wait_ge(S["ao_ev"], KD)
            pe.wait_ge(S["x2_ev"], 2 * TB)
            for k in range(KD):
                last = mm(bank[0][0:LW, :], wr[:, k, :], h2T[:, k, :], start=(k == 0), stop=(k == KD - 1))
            last.then_inc(S["rt_mm"], 1)
            pe.wait_ge(S["rt_ev"], 1)
            for b in range(TB):
                last = tr(bank[1][:, b * LW:(b + 1) * LW], lgT[:, b * P:(b + 1) * P], ident[0:LW, 0:LW])
            last.then_inc(S["rt_mm"], 1)
            pe.wait_ge(S["m_ready"], 1)
            pe.wait_ge(S["wo_ev"], 2 * TB)
            flat = lambda a: a[:, :, :].rearrange("p b e -> p (b e)")
            mm(bank[2][:, 0:TB * NE], before[:], flat(Mb), start=True, stop=False)
            mm(bank[2][:, 0:TB * NE], ones_b[:], flat(Mpre), start=False, stop=True)
            mm(bank[3][:, 0:NE], ones_b[:], Mtot, start=True, stop=True).then_inc(S["rank_mm"], 1)
            pe.wait_ge(S["oh_ready"], 1)
            for cc in range(2 * TB):
                for hf in range(2):
                    last = mm(bank[4][64 * hf:64 * hf + 64, 0:2 * MAXT], ohlo[:, cc, :],
                              ohv[:, cc, :, hf * MAXT:(hf + 1) * MAXT], start=(cc == 0), stop=(cc == 2 * TB - 1))
            last.then_inc(S["tab_mm"], 1)

            def transpose_tile(t):
                pe.wait_ge(S["xg_ready"], t + 1)
                view = xg.rearrange("p (q k) -> p k q", k=KD)
                for kh in range(2):
                    for kk in range(4):
                        last = tr(bank[6 + kh][:, kk * P:(kk + 1) * P], view[:, 4 * kh + kk, :], ident[:])
                    last.then_inc(S["xg_mm"], 1)

            pe.wait_ge(S["x2_ev"], 2 * TB)
            transpose_tile(0)
            with pe.Fori(0, PAIRS // 2) as i:
                for slot in range(2):
                    first = pe.value_load(tab[0:1, bass.ds(2 * i + slot, 1)], min_val=0, max_val=MAXT - 1)
                    end = pe.value_load(tab[0:1, bass.ds(2 * i + (slot + 1), 1)], min_val=1, max_val=MAXT - 1)
                    with pe.Fori(first, end) as t:
                        pe.wait_ge(ld_gu[slot], 64 * i + 64)
                        pe.wait_ge(S["xtev_a"], t + 1)
                        pe.wait_ge(S["xtev_v"], t + 1)
                        pe.wait_ge(S["hid_ready"], t + 1)
                        for k in range(KD):
                            for e in range(2):
                                last = mm(bank[0][64 * e:64 * e + 64, :], xTs[:, k, 64 * e:64 * e + 64],
                                          w_gu[slot][:, e, :, k, :], start=(k == 0), stop=(k == KD - 1))
                        last.then_inc(S["gu_mm"], 1)
                        transpose_tile(t + 1)
                        pe.wait_ge(S["hid_ready"], t + 2)
                        pe.wait_ge(S["hidT_ev"], t + 1)
                        view = hid.rearrange("p (q j) -> p j q", j=2)
                        for j in range(2):
                            last = tr(bank[1][:, j * P:(j + 1) * P], view[:, j, :], ident[:])
                        last.then_inc(S["hidT_mm"], 1)
                        pe.wait_ge(S["hidT_ev"], t + 2)
                        pe.wait_ge(S["yev_a"], t + 1)
                        pe.wait_ge(S["yev_v"], t + 1)
                        pe.wait_ge(ld_dn[slot], 32 * i + 32)
                        for n in range(2):
                            for j in range(2):
                                for e in range(2):
                                    last = mm(bank[2 + n][64 * e:64 * e + 64, :], hidT[:, j, 64 * e:64 * e + 64],
                                              w_dn[slot][:, e, j, n * BANK:(n + 1) * BANK],
                                              start=(j == 0), stop=(j == 1))
                            last.then_inc(S["y_mm"], 1)

        @block.scalar
        def _(act):
            a = nc.scalar.activation
            act.dma_start(cvrow[0:TAPS, :], conv_w[0]).then_inc(ld_rows, 16)
            act.dma_start(cvrow[TAPS:TAPS + 1, :], conv_b).then_inc(ld_rows, 16)
            act.dma_start(cvrow[TAPS + 1:TAPS + 2, :], conv_ln_g).then_inc(ld_rows, 16)
            act.dma_start(cvrow[TAPS + 2:TAPS + 3, :], conv_ln_b).then_inc(ld_rows, 16)
            act.dma_start(gmix[:], g_mix[0].rearrange("(p k) -> p k", k=KD)).then_inc(ld_gmix, 16)
            with nc.allow_non_contiguous_dma(reason="32 x 8 values"):
                act.dma_start(relbT[:], rel_bias.rearrange("k h -> h k")).then_inc(ld_relb, 16)
            act.dma_start(wsm, w_in2[:, :, KI0:GATE0]).then_inc(ld_small, 16)
            act.dma_start(wr_g[:], w_gr[0].rearrange("(p k) g -> p k g", k=KD)).then_inc(ld_router, 16)
            act.dma_start(wr_e[:], w_er[0].rearrange("g (p k) e -> p g (k e)", k=KD)).then_inc(ld_router, 16)
            act.dma_start(br[:, 0:NG], b_gr.to_broadcast([P, NG])).then_inc(ld_router, 16)
            act.dma_start(br[:, NG:LW], b_er.rearrange("a g e -> a (g e)").to_broadcast([P, NE]))\
                .then_inc(ld_router, 16)

            for b in range(TB):
                act.wait_ge(ld_x[b], 16)
                a(gflat[:, b * D:(b + 1) * D], xr[:, b, :], ACT.Square, accum_out=ss[:, 0, b:b + 1])\
                    .then_inc(S["ss_done"], 1)
            act.wait_ge(S["cv_mm"], 1)
            a(cv[:, :, :].rearrange("p c n -> p (c n)"), bank[0][:, 0:CC * (TAPS + 3)], ACT.Copy)\
                .then_inc(S["proj_ev"], 1)
            for j in range(4):
                act.wait_ge(S["proj_mm"], j + 1)
                a(glu[:, j, PAD:PAD + T], bank[j % 2][:], ACT.Copy).then_inc(S["proj_ev"], 1)
            for c in range(4):
                act.wait_ge(S["proj_mm"], 5 + c)
                if c >= 2:
                    act.wait_ge(S["glu_done"], c - 1)
                a(sig[:, c % 2, :], bank[c % 2][:], ACT.Sigmoid).then_inc(S["proj_ev"], 1)
            for j in range(4):
                act.wait_ge(S["proj_mm"], 9 + j)
                a(qT[:, j, :], bank[j % 2][:], ACT.Copy, scale=HEAD_DIM ** -0.5).then_inc(S["proj_ev"], 1)
            act.wait_ge(S["proj_mm"], 13)
            for gr in range(2):
                for lo in range(2):
                    last = a(kT[64 * lo:64 * lo + 64, gr, :], bank[0][64 * gr:64 * gr + 64, :], ACT.Copy)
            last.then_inc(S["proj_ev"], 1)
            act.wait_ge(S["proj_mm"], 14)
            a(vT[:], bank[1][:], ACT.Copy).then_inc(S["proj_ev"], 1)
            for j in range(2):
                act.wait_ge(S["proj_mm"], 15 + j)
                a(qiT[:, j, :], bank[j][:], ACT.Copy).then_inc(S["proj_ev"], 1)
            act.wait_ge(S["proj_mm"], 17)
            for i in range(4):
                a(kiT[32 * i:32 * i + 32, :], bank[0][0:ID, :], ACT.Copy)
            a(wiT, bank[0][ID:ID + IH, :], ACT.Copy).then_inc(S["proj_ev"], 1)
            act.wait_ge(S["vt_mm"], 1)
            a(wi[:, :, :].rearrange("p b h -> p (b h)"), bank[7][:, 0:TB * IH], ACT.Copy,
              scale=float(ID * IH) ** -0.5).then_inc(S["vt_ev"], 1)
            act.wait_ge(S["vt_mm"], 2)
            a(vrow[:, :, :].rearrange("p b n -> p (b n)"), bank[6][:], ACT.Copy).then_inc(S["vt_ev"], 1)
            act.wait_ge(S["xt_mm"], 2 * TB)
            for b in range(1, TB):
                n = P * (b + 1)
                for h in range(IH):
                    turn = (b - 1) * IH + h
                    act.wait_ge(S["ix_mm"], turn + 1)
                    o = relu_off[b] + h * n
                    a(r1[:, o:o + n], bank[2 + h % 4][:, 0:n], ACT.Relu).then_inc(S["ix_relu"], 1)
            with act.Fori(0, 2) as i:
                for q in range(8):
                    act.wait_ge(S["proj_mm"], 8 * i + (18 + q))
                    a(gflat[:, bass.ds((8 * i + q) * T, T)], bank[(q + 1) % 2][:], ACT.Sigmoid)\
                        .then_inc(S["proj_ev"], 1)
            for c in range(CC):
                act.wait_ge(S["yc_ready"], c + 1)
                a(sT[:, c, :], yv[:, c, :], ACT.Square).then_inc(S["sq_ready"], 1)
            act.wait_ge(S["lnvar_ready"], 1)
            a(work[:], score[:], ACT.Sqrt).then_inc(S["lnstd_ready"], 1)
            for c in range(CC):
                act.wait_ge(S["z_ready"], c + 1)
                a(sT[:, c, :], yv[:, c, :], ACT.Silu, scale=cv[:, c, TAPS + 1:TAPS + 2],
                  bias=cv[:, c, TAPS + 2:TAPS + 3]).then_inc(S["silu_ready"], 1)
            def exps(i):
                n = P * (attn[i][0] + 1)
                act.wait_ge(S["nm_ready"], i + 1)
                for r in range(4):
                    last = a(prob[i % 2][:, r, 0:n], prob[i % 2][:, r, 0:n], ACT.Exp, bias=nm[:, i % 2, r:r + 1],
                             accum_out=sm[:, i % 2, r:r + 1])
                last.then_inc(S["ex_done"], 1)

            exps(0)
            for i, (b, gr) in enumerate(attn):
                if i:
                    act.wait_ge(S["pv_mm"], i)
                for s in range(b + 1):
                    n = tiles_before[i] + s
                    act.wait_ge(S["pt_mm"], n + 1)
                    a(pT[:, s, :, :].rearrange("p r n -> p (r n)"), bank[6 + n % 2][:], ACT.Copy)\
                        .then_inc(S["pt_ev"], 1)
                if i + 1 < len(attn):
                    exps(i + 1)
            for b in range(TB):
                act.wait_ge(S["wo_ev"], 2 * b + 2)
                a(conv_buf[:, 2 * b:2 * b + 2, :].rearrange("p k n -> p (k n)"), xr[:, b, :], ACT.Square,
                  accum_out=ss[:, 1, b:b + 1]).then_inc(S["ss_done"], 1)
            act.wait_ge(S["ss_done"], 2 * TB)
            for n in range(2 * TB):
                act.wait_ge(S["x2_mm"], n + 1)
                b, kh = n // 2, n % 2
                a(h2T[:, 4 * kh:4 * kh + 4, b * P:(b + 1) * P],
                  bank[6 + n % 2][:].rearrange("p (k n) -> p k n", k=4), ACT.Copy).then_inc(S["x2_ev"], 1)
            act.wait_ge(S["rt_mm"], 1)
            a(lgT, bank[0][0:LW, :], ACT.Copy).then_inc(S["rt_ev"], 1)
            act.wait_ge(S["exp_in"], 1)
            a(gw[:, 1, :, 0:NG], gw[:, 0, :, 0:NG], ACT.Exp).then_inc(S["exp_out"], 1)
            act.wait_ge(S["exp_in"], 2)
            a(gs[:, 8, :], gs[:, 7, :], ACT.Exp).then_inc(S["exp_out"], 1)
            act.wait_ge(S["tab_ready"], 1)
            act.wait_ge(S["wo_mm"], 2 * TB)

            def rows_T(t):
                act.wait_ge(S["xg_mm"], 2 * t + 1)
                a(xTs[:, 0:4, :].rearrange("p k n -> p (k n)"), bank[6][:], ACT.Copy).then_inc(S["xtev_a"], 1)

            tiles = act.value_load(tab[0:1, PAIRS:PAIRS + 1], min_val=PAIRS, max_val=MAXT - 1)
            rows_T(0)
            with act.Fori(0, tiles) as t:
                act.wait_ge(S["gu_mm"], t + 1)
                act.wait_ge(S["hid_ready"], t + 1)
                a(sil, bank[0][:, 0:FF], ACT.Silu).then_inc(S["silu_g"], 1)
                rows_T(t + 1)
                act.wait_ge(S["y_mm"], 2 * t + 2)
                act.wait_ge(S["ys_free"], t + 1)
                a(ys[:, t % 2, BANK:2 * BANK], bank[3][:], ACT.Copy).then_inc(S["yev_a"], 1)
            for b in range(TB):
                act.wait_ge(S["y_add"], 2 * b + 2)
                a(conv_buf[:, 2 * b:2 * b + 2, :].rearrange("p k n -> p (k n)"), xr[:, b, :], ACT.Square,
                  accum_out=ss[:, 2, b:b + 1]).then_inc(S["ss_done"], 1)

        @block.vector
        def _(dve):
            v = nc.vector
            done = [0]

            def link(ins):
                done[0] += 1
                ins.then_inc(S["dve_chain"], 1)
                dve.wait_ge(S["dve_chain"], done[0])

            def mean_square(which, b):
                dve.wait_ge(S["ss_done"], TB * which + b + 1)
                v.tensor_scalar(ss[:, which, b:b + 1], ss[:, which, b:b + 1], 1.0 / D, EPS, ALU.mult, ALU.add)\
                    .then_inc(S["var_ready"], 1)
                dve.wait_ge(S["rstd_ready"], TB * which + b + 1)

            dve.wait_ge(ld_gmix, 16)

            def hT_out(n):
                dve.wait_ge(S["xt_mm"], n + 1)
                b, kh = n // 2, n % 2
                v.tensor_tensor(hT[:, 4 * kh:4 * kh + 4, b * P:(b + 1) * P],
                                bank[6 + n % 2][:].rearrange("p (k n) -> p k n", k=4),
                                spread(gmix[:, 4 * kh:4 * kh + 4], 2, P), ALU.mult).then_inc(S["xt_ev"], 1)

            for b in range(TB):
                mean_square(0, b)
                v.tensor_scalar(hrow[:, b, :], xr[:, b, :], rs[:, 0, b:b + 1], None, ALU.mult)\
                    .then_inc(S["h_ready"], 1)
                if b:
                    hT_out(2 * b - 2)
                    hT_out(2 * b - 1)
            hT_out(2 * TB - 2)
            hT_out(2 * TB - 1)
            dve.wait_ge(ld_relb, 16)
            dve.wait_ge(S["consts_ready"], 1)
            for lo, hi_, k in bucket_runs(-(P - 1), T - 1):
                last = v.tensor_copy(gdist[:, T - 1 - hi_:T - lo], relbT[:, k:k + 1].to_broadcast([H, hi_ - lo + 1]))
            last.then_inc(S["g_ready"], 1)
            for c in range(CC):
                dve.wait_ge(S["proj_ev"], 7 + c)
                v.tensor_tensor(glu[:, c, PAD:PAD + T], glu[:, c, PAD:PAD + T], sig[:, c % 2, :], ALU.mult)\
                    .then_inc(S["glu_done"], 1)
            dve.wait_ge(S["glu_done"], CC)
            TAPU = 3
            for c0 in range(0, CC, 2):
                base = c0 // 2 * 2 * TAPS
                for c in (c0, c0 + 1):
                    v.tensor_scalar(yv[:, c, :], glu[:, c, 0:T], cv[:, c, 0:1], cv[:, c, TAPS:TAPS + 1],
                                    ALU.mult, ALU.add).then_inc(S["conv_step"], 1)
                with dve.Fori(0, (TAPS - 1) // TAPU) as i:
                    for u in range(TAPU):
                        for c in (c0, c0 + 1):
                            dve.wait_ge(S["conv_step"], i * (2 * TAPU) + (base + 2 * u + (c - c0) + 1))
                            v.scalar_tensor_tensor(yv[:, c, :], glu[:, c, bass.ds(i * TAPU + (u + 1), T)],
                                                   cv[:, c, bass.ds(i * TAPU + (u + 1), 1)], yv[:, c, :],
                                                   ALU.mult, ALU.add).then_inc(S["conv_step"], 1)
            dve.wait_ge(S["conv_step"], CC * TAPS)
            link(v.memset(m8[:], 0.0))
            v.memset(m8[:], 0.0).then_inc(S["conv_ready"], 1)
            dve.wait_ge(S["conv_ready"], 1)
            for b in range(1, TB):
                n = P * (b + 1)
                dve.wait_ge(S["vt_ev"], 2)
                for h in range(IH):
                    dve.wait_ge(S["ix_relu"], (b - 1) * IH + h + 1)
                    o = relu_off[b] + h * n
                    w = wi[:, b, h:h + 1]
                    if h == 0:
                        link(v.tensor_scalar(score[:, 0:n], r1[:, o:o + n], w, None, ALU.mult))
                    else:
                        link(v.scalar_tensor_tensor(score[:, 0:n], r1[:, o:o + n], w, score[:, 0:n],
                                                    ALU.mult, ALU.add))
                link(v.memset(score[0:CHUNK, n - CHUNK:n], NEG))
                src = score
                for _ in range(TOPK // 8):
                    link(v.max(m8[:], src[:, 0:n]))
                    link(v.match_replace(work[:, 0:n], m8[:], src[:, 0:n], NEG))
                    src = work
                link(v.tensor_tensor(work[:, 0:n], work[:, 0:n], score[:, 0:n], ALU.is_equal))
                v.tensor_scalar(mask[:, MOFF[b]:MOFF[b] + n], work[:, 0:n], MASKED, None, ALU.mult)\
                    .then_inc(S["mask_ready"], 1)
            dve.wait_ge(S["ln_mm"], 1)
            for c in range(CC):
                v.scalar_tensor_tensor(yv[:, c, :], bank[6][:], -1.0 / C, yv[:, c, :], ALU.mult, ALU.add)\
                    .then_inc(S["yc_ready"], 1)
            dve.wait_ge(S["ln_mm"], 2)
            dve.wait_ge(S["mask_ready"], TB - 1)
            v.tensor_scalar(score[:], bank[7][:], 1.0 / C, EPS, ALU.mult, ALU.add).then_inc(S["lnvar_ready"], 1)
            dve.wait_ge(S["lnstd_ready"], 1)
            link(v.reciprocal(work[:], work[:]))
            link(v.tensor_tensor(score[:], score[:], work[:], ALU.mult))
            link(v.tensor_tensor(score[:], score[:], work[:], ALU.mult))
            link(v.tensor_scalar(score[:], score[:], -0.5, 1.5, ALU.mult, ALU.add))
            link(v.tensor_tensor(work[:], score[:], work[:], ALU.mult))
            for c in range(CC):
                v.tensor_tensor(yv[:, c, :], yv[:, c, :], work[:], ALU.mult).then_inc(S["z_ready"], 1)
            for n in range(KD):
                dve.wait_ge(S["co_mm"], n + 1)
                v.tensor_tensor(gA[:, n, :], gA[:, n, :], bank[n % 2][:], ALU.mult).then_inc(S["co_ev"], 1)

            def logits_out(i):
                n = P * (attn[i][0] + 1)
                if i >= 2:
                    dve.wait_ge(S["pt_mm"], tiles_before[i - 1])
                for r in range(4):
                    dve.wait_ge(S["qk_mm"], 4 * i + r + 1)
                    dve.wait_ge(S["bm_ready"], 4 * i + r + 1)
                    v.tensor_tensor_reduce(out=prob[i % 2][:, r, 0:n], in0=bank[2 + r][:, 0:n],
                                           in1=bm[:, r % 2, 0:n], scale=1.0, scalar=NEG, op0=ALU.add, op1=ALU.max,
                                           accum_out=mx[:, i % 2, r:r + 1]).then_inc(S["lg_done"], 1)
                dve.wait_ge(S["lg_done"], 4 * i + 4)
                v.tensor_scalar(nm[:, i % 2, :], mx[:, i % 2, :], -1.0, None, ALU.mult).then_inc(S["nm_ready"], 1)

            def outputs_out(i):
                b, gr = attn[i]
                dve.wait_ge(S["pv_mm"], i + 1)
                v.tensor_copy(oT[:, 2 * gr:2 * gr + 2, b * P:(b + 1) * P],
                              bank[i % 2][:, 0:2 * P].rearrange("p (j n) -> p j n", j=2)).then_inc(S["ot_ev"], 1)

            logits_out(0)
            for i, (b, gr) in enumerate(attn):
                n = P * (b + 1)
                dve.wait_ge(S["ex_done"], i + 1)
                link(v.reciprocal(ri[:, i % 2, :], sm[:, i % 2, :]))
                for r in range(4):
                    last = v.tensor_scalar(prob[i % 2][:, r, 0:n], prob[i % 2][:, r, 0:n], ri[:, i % 2, r:r + 1],
                                           None, ALU.mult)
                last.then_inc(S["p_ready"], 1)
                if i + 1 < len(attn):
                    logits_out(i + 1)
                if i:
                    outputs_out(i - 1)
            outputs_out(len(attn) - 1)
            for n in range(KD):
                dve.wait_ge(S["ao_mm"], n + 1)
                v.tensor_tensor(gB[:, n, :], gB[:, n, :], bank[n % 2][:], ALU.mult).then_inc(S["ao_ev"], 1)
                dve.wait_ge(S["ao_ev"], n + 1)
                v.tensor_tensor(gA[:, n, :], gA[:, n, :], gB[:, n, :], ALU.add).then_inc(S["merged"], 1)
            dve.wait_ge(ld_router, 64)
            v.tensor_copy(wr[:, :, 0:NG], wr_g[:])
            for gr in range(NG):
                last = v.tensor_copy(wr[:, :, NG + gr * EG:NG + (gr + 1) * EG], wr_e[:, gr, :, :])
            last.then_inc(S["wr_ready"], 1)
            dve.wait_ge(ld_gbc, 32)
            dve.wait_ge(S["merged"], KD)

            def residual(b):
                for hf in range(2):
                    m = 2 * b + hf
                    dve.wait_ge(S["wo_mm"], m + 1)
                    v.tensor_tensor(xr[:, b, hf * BANK:(hf + 1) * BANK], xr[:, b, hf * BANK:(hf + 1) * BANK],
                                    bank[2 + m % 4][:], ALU.add).then_inc(S["wo_ev"], 1)

            residual(0)
            for b in range(TB):
                if b + 1 < TB:
                    residual(b + 1)
                mean_square(1, b)
                v.scalar_tensor_tensor(h2row[:, b, :], xr[:, b, :], rs[:, 1, b:b + 1], g_bc[:, 0, :],
                                       ALU.mult, ALU.mult).then_inc(S["h2_ready"], 1)
            dve.wait_ge(S["rt_mm"], 2)
            link(v.tensor_tensor(lg, bank[1][:, 0:TB * LW].rearrange("p (b n) -> p b n", b=TB),
                                 spread(br[:], 1, TB), ALU.add))
            dve.wait_ge(S["consts_ready"], 2)

            def first_max(val, d, mxo, eqw, one, n):
                link(v.tensor_reduce(mxo, val, AX, ALU.max))
                link(v.tensor_tensor(d, val, spread(mxo, 2, n), ALU.subtract))
                link(v.scalar_tensor_tensor(eqw, d, 0.0, spread(rev[:, EG - n:EG], 1, TB), ALU.is_equal, ALU.mult))
                link(v.tensor_reduce(gs[:, 0, :], eqw, AX, ALU.max))
                link(v.tensor_tensor(one, eqw, spread(gs[:, 0, :], 2, n), ALU.is_equal))

            first_max(lg[:, :, 0:NG], gw[:, 0, :, 0:NG], gs[:, 1, :], gw[:, 2, :, 0:NG], gw[:, 3, :, 0:NG], NG)
            v.memset(gs[:, 15, :], 0.0).then_inc(S["exp_in"], 1)
            oneg = gw[:, 3, :, 0:NG]
            link(v.tensor_tensor(e4, lg[:, :, NG:LW].rearrange("p b (g e) -> p b g e", g=NG),
                                 spread(oneg, 3, EG), ALU.mult))
            link(v.tensor_reduce(gw[:, 4, :, :], e4[:, :, :, :].rearrange("p b g e -> p b e g"), AX, ALU.add))
            first_max(gw[:, 4, :, :], gw[:, 5, :, :], gs[:, 2, :], gw[:, 6, :, :], gw[:, 7, :, :], EG)
            link(v.scalar_tensor_tensor(gw[:, 8, :, :], gw[:, 7, :, :], NEG, gw[:, 4, :, :], ALU.mult, ALU.add))
            first_max(gw[:, 8, :, :], gw[:, 9, :, :], gs[:, 3, :], gw[:, 10, :, :], gw[:, 11, :, :], EG)
            v.tensor_tensor(gs[:, 7, :], gs[:, 3, :], gs[:, 2, :], ALU.subtract).then_inc(S["exp_in"], 1)
            for c, one in enumerate((gw[:, 7, :, :], gw[:, 11, :, :])):
                link(v.tensor_tensor(Mf[:, c, :, :].rearrange("p b (g e) -> p b g e", g=NG),
                                     spread(oneg, 3, EG), spread(one, 2, NG), ALU.mult))
            link(v.tensor_tensor(Mb, Mf[:, 0, :, :], Mf[:, 1, :, :], ALU.add))
            link(v.memset(Mpre[:, 0, :], 0.0))
            for b in range(1, TB):
                link(v.tensor_tensor(Mpre[:, b, :], Mpre[:, b - 1, :], Mb[:, b - 1, :], ALU.add))
            v.tensor_tensor(Mtot, Mpre[:, TB - 1, :], Mb[:, TB - 1, :], ALU.add).then_inc(S["m_ready"], 1)
            dve.wait_ge(S["exp_out"], 2)
            link(v.tensor_reduce(gs[:, 4, :], gw[:, 1, :, 0:NG], AX, ALU.add))
            link(v.tensor_scalar(gs[:, 5, :], gs[:, 8, :], 1.0, None, ALU.add))
            link(v.tensor_tensor(gs[:, 6, :], gs[:, 4, :], gs[:, 5, :], ALU.mult))
            link(v.reciprocal(wts[:, 0, :], gs[:, 6, :]))
            link(v.tensor_tensor(wts[:, 1, :], wts[:, 0, :], gs[:, 8, :], ALU.mult))
            dve.wait_ge(S["rank_mm"], 1)
            link(v.tensor_scalar(cnti[:], bank[3][:, 0:NE], float(SLOTS - 1), None, ALU.add))
            link(v.tensor_scalar(cnti[:], cnti[:], 6, None, ALU.arith_shift_right))
            link(v.tensor_copy(cnt[:], cnti[:]))
            pairs = cnt[:].rearrange("p (q e) -> p q e", e=2)
            link(v.tensor_reduce(nseg[:], pairs, AX, ALU.max))
            link(v.tensor_scalar(nseg[:], nseg[:], 1.0, None, ALU.max))
            link(v.tensor_tensor_scan(tend[:], ones[:, 0:PAIRS], nseg[:], 0.0, ALU.mult, ALU.add))
            link(v.memset(tab[:, 0:1], 0))
            v.tensor_copy(tab[:, 1:PAIRS + 1], tend[:]).then_inc(S["tab_ready"], 1)
            link(v.tensor_tensor(nseg[:], tend[:], nseg[:], ALU.subtract))
            link(v.tensor_tensor(hib[:].rearrange("p (q e) -> p q e", e=2), spread(nseg[:], 2, 2),
                                 half32[:].rearrange("p (q e) -> p q e", e=2), ALU.add))
            link(v.tensor_copy(posr[:, :, :].rearrange("p b e -> p (b e)"), bank[2][:, 0:TB * NE]))
            for c in range(2):
                link(v.tensor_tensor(big[:, c, :, :], Mf[:, c, :, :], posr, ALU.mult))
            link(v.tensor_reduce(posc[:], big[:, :, :, :].rearrange("p c b e -> p (c b) e"), AX, ALU.add))
            for c in range(2):
                link(v.tensor_tensor(big[:, c, :, :], Mf[:, c, :, :], spread(hib[:], 1, TB), ALU.mult))
            link(v.tensor_reduce(hic[:], big[:, :, :, :].rearrange("p c b e -> p (c b) e"), AX, ALU.add))
            link(v.tensor_copy(posi[:], posc[:]))
            link(v.tensor_scalar(loi[:], posi[:], SLOTS - 1, None, ALU.bitwise_and))
            link(v.tensor_scalar(segi[:], posi[:], 6, None, ALU.arith_shift_right))
            link(v.tensor_tensor(hi[:], segi[:], hic[:], ALU.add))
            link(v.tensor_copy(posc[:], loi[:]))
            link(v.tensor_tensor(ohlo, spread(iota64[:], 1, 2 * TB), spread(posc[:], 2, 64), ALU.is_equal))
            link(v.tensor_tensor(ohhi, spread(iota64[:], 1, 2 * TB), spread(hi[:], 2, 64), ALU.is_equal))
            link(v.tensor_scalar(ohv[:, :, 0, :], ohhi, part1[:], None, ALU.mult))
            v.tensor_tensor(ohv[:, :, 1, :], ohhi, spread(blkcode[:], 2, 64), ALU.mult).then_inc(S["oh_ready"], 1)
            dve.wait_ge(S["tab_mm"], 1)
            link(v.tensor_scalar(inv[:], bank[4][:, 0:MAXT], 0.0, float(BIG_ROW), ALU.is_equal, ALU.mult))
            link(v.tensor_copy(dst[:], bank[4][:, MAXT:2 * MAXT]))
            link(v.tensor_tensor(dst[:], bank[4][:, 0:MAXT], dst[:], ALU.add))
            link(v.tensor_scalar(dst[:], dst[:], -1.0, 0.0, ALU.add, ALU.max))
            link(v.tensor_copy(dsti[:], dst[:]))
            link(v.tensor_scalar(toki[:], dsti[:], T - 1, None, ALU.bitwise_and))
            link(v.tensor_tensor(sidx[:], dst[:], inv[:], ALU.add))
            link(v.memset(gidx[:, MAXT:MAXT + RING + 1], BIG_ROW))
            v.tensor_tensor(gidx[:, 0:MAXT], toki[:], inv[:], ALU.add).then_inc(S["tab_ready"], 1)

            def rows_T(t):
                dve.wait_ge(S["xg_mm"], 2 * t + 2)
                v.tensor_copy(xTs[:, 4:8, :].rearrange("p k n -> p (k n)"), bank[7][:]).then_inc(S["xtev_v"], 1)

            dve.wait_ge(S["tab_ready"], 2)
            tiles = dve.value_load(tab[0:1, PAIRS:PAIRS + 1], min_val=PAIRS, max_val=MAXT - 1)
            rows_T(0)
            with dve.Fori(0, tiles) as t:
                dve.wait_ge(S["silu_g"], t + 1)
                dve.wait_ge(S["hidT_mm"], t + 1)
                v.tensor_tensor(hid, sil, bank[0][:, FF:2 * FF], ALU.mult).then_inc(S["hid_ready"], 1)
                rows_T(t + 1)
                dve.wait_ge(S["hidT_mm"], t + 2)
                v.tensor_copy(hidT[:, :, :].rearrange("p j n -> p (j n)"), bank[1][:, 0:2 * P])\
                    .then_inc(S["hidT_ev"], 1)
                dve.wait_ge(S["y_mm"], 2 * t + 1)
                dve.wait_ge(S["ys_free"], t + 1)
                v.tensor_copy(ys[:, t % 2, 0:BANK], bank[2][:]).then_inc(S["yev_v"], 1)
            for b in range(TB):
                dve.wait_ge(ld_y[b % 2], 32 * (b // 2) + 32)
                for c in range(2):
                    v.scalar_tensor_tensor(xr[:, b, :], yrow[:, 2 * (b % 2) + c, :], wts[:, c, b:b + 1], xr[:, b, :],
                                           ALU.mult, ALU.add).then_inc(S["y_add"], 1)
                    dve.wait_ge(S["y_add"], 2 * b + c + 1)
            for b in range(TB):
                mean_square(2, b)
                v.scalar_tensor_tensor(xr[:, b, :], xr[:, b, :], rs[:, 2, b:b + 1], g_bc[:, 1, :],
                                       ALU.mult, ALU.mult).then_inc(S["o_ready"], 1)


_INS = ["x", "g_mix", "w_in", "conv_w", "conv_b", "conv_ln_g", "conv_ln_b", "w_conv_out", "w_attn_out", "w_out",
        "rel_bias", "g_ffn", "w_group_router", "b_group_router", "w_expert_router", "b_expert_router",
        "w_e_gate", "w_e_up", "w_e_down", "g_final"]


def kernel(**inputs):
    import concourse.bacc as bacc
    from concourse.bass_utils import run_bass_kernel_spmd

    nc = bacc.Bacc("TRN2", target_bir_lowering=False, num_devices=1)
    arrays, args = {}, []
    for name in _INS:
        a = np.ascontiguousarray(inputs[name])
        arrays[f"in_{name}"] = a
        args.append(nc.dram_tensor(f"in_{name}", a.shape, mybir.dt.from_np(a.dtype), kind="ExternalInput").ap())
    shape = tuple(inputs["x"].shape)
    args.append(nc.dram_tensor("out_0", shape, F32, kind="ExternalOutput").ap())
    build(nc, *args)
    r = run_bass_kernel_spmd(nc, [arrays], core_ids=[0])
    return r.results[0]["out_0"]
```

```python
from contextlib import ExitStack

import numpy as np

import concourse.bass as bass
from concourse import mybir

F32 = mybir.dt.float32
BF16 = mybir.dt.bfloat16
F32R = mybir.dt.float32r
I32 = mybir.dt.int32
U32 = mybir.dt.uint32
ALU = mybir.AluOpType
ACT = mybir.ActivationFunctionType
AX = mybir.AxisListType.X

P = 128
BANK = 512
NEG = -3.0e38
MASKED = -1.0e30
EPS = 1e-6
CHUNK = 64
HEAD_DIM = 64
TOPK = 128
BIG_ROW = 4096

BUCKET_STARTS = [0, 1, 2, 3, 4, 5, 6, 7, 8, 12, 16, 23, 32, 46, 64, 91]


def bucket_runs(lowest, highest):
    ends = [s - 1 for s in BUCKET_STARTS[1:]] + [1 << 20]
    runs = []
    for k in range(15, -1, -1):
        runs.append((-ends[k], -max(BUCKET_STARTS[k], 1), 16 + k))
    for k in range(16):
        runs.append((BUCKET_STARTS[k], ends[k], k))
    clipped = [(max(a, lowest), min(b, highest), k) for a, b, k in runs]
    return [(a, b, k) for a, b, k in clipped if a <= b]


def spread(ap, axis, n):
    shape = list(ap.shape)
    shape.insert(axis, n)
    return ap.unsqueeze(axis).to_broadcast(shape)


def build(nc, x, g_mix, w_in, conv_w, conv_b, conv_ln_g, conv_ln_b, w_conv_out, w_attn_out, w_out,
          rel_bias, g_ffn, w_gr, b_gr, w_er, b_er, w_e_gate, w_e_up, w_e_down, g_final, out):
    _, T, D = x.shape
    TB = T // P
    KD = D // P
    C = conv_w.shape[2]
    CC = C // P
    TAPS = conv_w.shape[1]
    PAD = TAPS - 1
    H = rel_bias.shape[1]
    NG, EG = w_er.shape[1], w_er.shape[3]
    NE = NG * EG
    FF = w_e_gate.shape[3]
    SLOTS = 64
    PAIRS = NE // 2
    RING = 4
    MAXT = 32
    assert PAIRS + (2 * T - PAIRS) // SLOTS < MAXT
    IH, ID = 8, 32
    LW = NG + NE
    QI0 = 2 * C + H * HEAD_DIM + 2 * P
    KI0 = QI0 + IH * ID
    GATE0 = KI0 + ID + IH
    NSMALL = ID + IH

    h2_dram = nc.dram_tensor("h2_rows", (T, D), F32).ap()
    y_dram = nc.dram_tensor("expert_rows", (2 * T, D), F32).ap()
    bias_dram = nc.dram_tensor("bias_by_distance", (H, P, 640), F32).ap()

    with ExitStack() as ctx:
        def sb(name, shape, dt=F32):
            return ctx.enter_context(nc.sbuf_tensor(name, shape, dt))

        def sem(name):
            return ctx.enter_context(nc.semaphore(name))

        bank = [ctx.enter_context(nc.psum_tensor(f"bank{i}", [P, BANK], F32)) for i in range(8)]

        REG = 2 * 3 * 2048
        r0 = sb("region0", [P, REG])
        r0_at = nc.sbuf_base - 4 * REG
        r1 = sb("region1", [P, REG])
        r1_at = nc.sbuf_base - 4 * REG
        region = [r0, r1]
        win = [r0[:, s * 2048:(s + 1) * 2048].rearrange("p (k n) -> p k n", k=KD) for s in range(2)]
        relu = r0[:, 4096:8192].rearrange("p (u n) -> p u n", u=8)
        prob = [r0[:, 4096 + s * 2048:6144 + s * 2048].rearrange("p (r n) -> p r n", r=4) for s in range(2)]
        wao = r0[:, 0:4096].rearrange("p (k n) -> p k n", k=CC)
        wco = r0[:, 8192:12288].rearrange("p (k n) -> p k n", k=CC)
        wout = [r0[:, o:o + 4096].rearrange("p (k n) -> p k n", k=KD) for o in (0, 8192)]
        hrow = r1[:, 0:4096].rearrange("p (b n) -> p b n", b=TB)
        bias = r1[:, 0:4096].rearrange("p (h n) -> p h n", h=H)

        w_gu = [r[:, 0:8192].rearrange("p (e m k f) -> p e m k f", e=2, m=2, k=KD) for r in region]
        w_dn = [r[:, 8192:12288].rearrange("p (e j n) -> p e j n", e=2, j=2) for r in region]

        xr = sb("x_rows", [P, TB, D])
        gates = sb("gates", [P, 2 * KD, T])
        gates_at = nc.sbuf_base - 4 * 2 * KD * T
        gA, gB = gates[:, 0:KD, :], gates[:, KD:2 * KD, :]
        h2row = gates[:, 0:KD, :].rearrange("p k n -> p (k n)").rearrange("p (b n) -> p b n", b=TB)

        def part(name, shape, at_):
            return nc.alloc_sbuf_tensor_at(name, shape, F32R, offset=at_).ap()

        h_hi = part("h_hi", [P, KD, T], r0_at + 4 * 8192)
        h_lo = part("h_lo", [P, KD, T], r1_at + 4 * 4096)
        w_part = part("w_part", [P, 2, 2, 1024], r1_at + 4 * 8192)
        qi_part = part("qi_part", [P, 2, 2, T], gates_at)
        ki_part = part("ki_part", [P, 2, T], gates_at + 4 * 2048)
        o_part = part("o_part", [P, 2, CC, T], r0_at + 4 * 4096)
        s_part = part("s_part", [P, 2, CC, T], r1_at + 4 * 4096)
        m_hi = part("m_hi", [P, KD, T], gates_at + 4 * 4096)
        m_lo = part("m_lo", [P, KD, T], r1_at)
        gflat = gates[:, :, :].rearrange("p k n -> p (k n)")
        xg = gflat[:, 0:1024]
        xTs = gflat[:, 1024:2048].rearrange("p (k n) -> p k n", k=KD)
        hid = gflat[:, 2048:2304]
        sil = gflat[:, 2304:2560]
        hidT = gflat[:, 2560:2816].rearrange("p (j n) -> p j n", j=2)
        ring = gflat[:, 4096:8192].rearrange("p (u n) -> p u n", u=RING)
        yrow = gflat.rearrange("p (u n) -> p u n", u=8)
        conv_buf = sb("conv_buf", [P, 2 * CC, T])
        yv, sT = conv_buf[:, 0:CC, :], conv_buf[:, CC:2 * CC, :]
        h2T = conv_buf
        ys = conv_buf[:, :, :].rearrange("p (u k) n -> p u (k n)", u=RING)
        pT = sT.rearrange("p s (r n) -> p s r n", r=4)
        sig = yv
        index_score = sT[:, 0, :]
        qT = sb("qT", [P, CC, T])
        oT = qT[:, :, :]
        g_bc = qT[:, :, :].rearrange("p k n -> p (k n)").rearrange("p (u n) -> p u n", u=2)
        kT = sb("kT", [P, 2, T])
        vrow = sb("v_rows", [P, TB, P])
        glu = sb("glu", [P, CC, PAD + T])
        bm = sb("bm", [P, 4, T])
        score, work = bm[:, 2, :], bm[:, 3, :]
        vT, wiT = bm[:, 1, :], bm[0:IH, 0, :]
        mask = sb("mask", [P, 1280])
        MOFF = [0, 128, 384, 768]

        ident = sb("ident", [P, P])
        ones = sb("ones", [P, P])
        ones_b = sb("ones_b", [P, P], BF16)
        before = sb("before", [P, P], BF16)
        iota64 = sb("iota64", [P, 64])
        part1 = sb("part1", [P, 1])
        blkcode = sb("blkcode", [P, 2 * TB])
        half32 = sb("half32", [P, NE])
        rev = sb("rev", [P, EG])
        mhalf = sb("mhalf", [P, 1])
        cvrow = gflat[0:TAPS + 3, 5504:5504 + C]
        cv = sb("cv", [P, CC, TAPS + 3])
        gmix = gflat[:, 4096:5120]
        relbT = sb("relbT", [H, 32])
        gdist = sb("gdist", [H, 640])
        wsm = gflat[:, 5120:5120 + KD * NSMALL].rearrange("p (k n) -> p k n", k=KD)
        wi = sb("wi", [P, TB, IH])
        ss = sb("ss", [P, 3, TB])
        rs = sb("rs", [P, 3, TB])
        m8 = sb("m8", [P, 8])
        mx = sb("mx", [P, 2, 4])
        nm = sb("nm", [P, 2, 4])
        sm = sb("sm", [P, 2, 4])
        ri = sb("ri", [P, 2, 4])
        wr = sb("wr", [P, KD, LW])
        wr_g = sb("wr_g", [P, KD, NG])
        wr_e = sb("wr_e", [P, NG, KD, EG])
        br = sb("br", [P, LW])
        gluf = glu[:, :, :].rearrange("p c n -> p (c n)")
        cut = [0]

        def piece(words):
            cut[0] += words
            return gluf[:, cut[0] - words:cut[0]]

        lg = piece(TB * LW).rearrange("p (b n) -> p b n", b=TB)
        gw = piece(12 * TB * EG).rearrange("p (u b n) -> p u b n", u=12, b=TB)
        gs = piece(16 * TB).rearrange("p (u b) -> p u b", u=16)
        e4 = piece(TB * NE).rearrange("p (b g e) -> p b g e", b=TB, g=NG)
        Mf = piece(2 * TB * NE).rearrange("p (c b e) -> p c b e", c=2, b=TB)
        Mb = mask[:, 768:832].bitcast(BF16).rearrange("p (b e) -> p b e", b=TB)
        Mpre = mask[:, 832:896].bitcast(BF16).rearrange("p (b e) -> p b e", b=TB)
        Mtot = mask[:, 896:912].bitcast(BF16)
        big = piece(4 * TB * NE).rearrange("p (u c b e) -> p u c b e", u=2, c=2, b=TB)
        cnt = sb("cnt", [P, NE])
        cnti = sb("cnti", [P, NE], I32)
        nseg = sb("nseg", [P, PAIRS])
        tend = sb("tend", [P, PAIRS])
        hib = sb("hib", [P, NE])
        tab = sb("tab", [P, PAIRS + 1], I32)
        posc = sb("posc", [P, 2 * TB])
        hic = sb("hic", [P, 2 * TB])
        posi = sb("posi", [P, 2 * TB], I32)
        loi = sb("loi", [P, 2 * TB], I32)
        segi = sb("segi", [P, 2 * TB], I32)
        hi = sb("hi", [P, 2 * TB])
        ohhi = piece(2 * TB * 64).rearrange("p (c n) -> p c n", c=2 * TB)
        ohlo = mask[:, 0:256].bitcast(BF16).rearrange("p (c n) -> p c n", c=2 * TB)
        ohv = mask[:, 256:768].bitcast(BF16).rearrange("p (c u n) -> p c u n", c=2 * TB, u=2)
        inv = sb("inv", [P, MAXT])
        dst = sb("dst", [P, MAXT])
        dsti = sb("dsti", [P, MAXT], I32)
        toki = sb("toki", [P, MAXT], I32)
        sidx = sb("sidx", [P, MAXT], U32)
        gidx = sb("gidx", [P, MAXT + RING + 1], U32)
        carrier = sb("carrier", [P, 6])
        gi1 = sb("gi1", [P, RING], U32)
        si1 = sb("si1", [P, RING], U32)
        wts = sb("wts", [P, 2, TB])

        ld_x = [sem(f"ld_x{b}") for b in range(TB)]
        ld_rows = sem("ld_rows")
        ld_gmix = sem("ld_gmix")
        ld_relb = sem("ld_relb")
        ld_win = [sem("ld_win0"), sem("ld_win1")]
        ld_small = sem("ld_small")
        ld_wco = sem("ld_wco")
        ld_wao = sem("ld_wao")
        ld_wout = [sem("ld_wout0"), sem("ld_wout1")]
        ld_router = sem("ld_router")
        ld_gbc = sem("ld_gbc")
        st_bias = sem("st_bias")
        ld_bias = sem("ld_bias")
        st_h2 = sem("st_h2")
        ld_gu = [sem("ld_gu0"), sem("ld_gu1")]
        ld_dn = [sem("ld_dn0"), sem("ld_dn1")]
        gathered = [sem(f"gathered{u}") for u in range(RING)]
        scattered = [sem(f"scattered{u}") for u in range(RING)]
        ld_y = [sem(f"ld_y{b}") for b in range(TB)]
        st_out = sem("st_out")
        names = """consts_ready ss_done var_ready rstd_ready h_ready cv_mm cv_ev xt_mm hhi_ready hlo_ready
            g_ready w_hi w_lo unit_mm unit_ev index_lo glu_done conv_step vt_mm vt_ev ix_mm ix_relu ix_acc
            mask_ready conv_ready ln_mm yc_ready sq_ready lnvar_ready lnstd_ready z_ready silu_ready s_hi s_lo
            bm_ready qk_mm lg_done nm_ready ex_done ri_ready p_ready pt_mm pt_ev pv_mm ot_ev o_hi o_lo gate_ready branch_ev
            merged m_hi m_lo wo_mm wo_ev h2_ready x2_mm x2_ev wr_ready
            rt_mm exp_in exp_out m_ready rank_mm oh_ready tab_mm tab_ready gu_half gu_mm silu_g hid_ready
            hidT_mm hidT_ev y_mm yev_a yev_v xg_mm xtev_a xtev_v idx_copy y_add o_scaled o_half o_ready dve_chain pool_chain
            ys_free rows_ready xg_ready sidx_copy""".split()
        S = {n: sem(n) for n in names}

        block = ctx.enter_context(nc.Block())
        pair_col = [c * P for c in (14, 12, 8, 10, 0, 2, 4, 6)] + [GATE0 + D + 2 * P * i for i in range(4)] \
            + [GATE0 + 2 * P * i for i in range(4)]
        assert QI0 == 14 * P
        NPROJ = 1 + 2 * len(pair_col)
        AO0, CO0, WO0 = NPROJ, NPROJ + KD, NPROJ + 2 * KD
        WO1 = WO0 + KD // 2
        NUNIT = WO0 + KD
        FREE0 = 21

        def unit_raw(u):
            if u == 0:
                return wsm
            if u < AO0:
                q = (u - 1) % 2
                return win[(u - 1) // 2 % 2][:, :, q * P:(q + 1) * P]
            if u < WO0:
                n = (u - AO0) % KD
                return (wao if u < CO0 else wco)[:, :, n * P:(n + 1) * P]
            hf, kp = divmod(u - WO0, 4)
            return wout[hf][:, 2 * kp:2 * kp + 2, :]

        def unit_part(u, part_):
            raw = unit_raw(u)
            k, n = raw.shape[1], raw.shape[2]
            if u >= WO1:
                q, r = divmod(u - WO1, 2)
                return (o_part, s_part)[q][:, r, 2 * part_:2 * part_ + 2, :]
            return w_part[:, u % 2, part_, 0:k * n].rearrange("p (k n) -> p k n", k=k)

        attn = [(b, g) for b in range(TB) for g in range(2)]
        tiles_before = [sum(b2 + 1 for b2, _ in attn[:i]) for i in range(len(attn) + 1)]
        units_a, units_b, nxt = [], [], FREE0
        for i in range(len(attn)):
            units_a.append(nxt)
            nxt += 1
            units_b.append(nxt if i % 2 else None)
            nxt += i % 2
        assert nxt == NPROJ

        def pt_bank(i, s):
            return 6 if s % 2 == 0 else (units_a[i] + 1) % 2

        def wo_bank(hf, b):
            return 2 + b if hf else (6, 7, 0, 1)[b]

        w_in2 = w_in[0].rearrange("(p k) n -> p k n", k=KD)

        @block.sync
        def _(sp):
            for b in range(TB):
                sp.dma_start(xr[:, b, :], x[0, b * P:(b + 1) * P, :]).then_inc(ld_x[b], 16)
            sp.dma_start(wsm, w_in2[:, :, KI0:GATE0]).then_inc(ld_small, 16)
            for p in range(len(pair_col)):
                if p >= 2:
                    sp.wait_ge(S["w_lo"], 2 * p - 1)
                sp.dma_start(win[p % 2], w_in2[:, :, pair_col[p]:pair_col[p] + 2 * P]).then_inc(ld_win[p % 2], 16)
                if p == 1:
                    sp.dma_start(cvrow[0:TAPS, :], conv_w[0]).then_inc(ld_rows, 16)
                    for i, w in enumerate((conv_b, conv_ln_g, conv_ln_b)):
                        sp.dma_start(cvrow[TAPS + i:TAPS + i + 1, :], w).then_inc(ld_rows, 16)
                    with nc.allow_non_contiguous_dma(reason="32 x 8 values"):
                        sp.dma_start(relbT[:], rel_bias.rearrange("k h -> h k")).then_inc(ld_relb, 16)
                    sp.dma_start(wr_g[:], w_gr[0].rearrange("(p k) g -> p k g", k=KD)).then_inc(ld_router, 16)
                    sp.dma_start(wr_e[:], w_er[0].rearrange("g (p k) e -> p g (k e)", k=KD)).then_inc(ld_router, 16)
                    sp.dma_start(br[:, 0:NG], b_gr.to_broadcast([P, NG])).then_inc(ld_router, 16)
                    sp.dma_start(br[:, NG:LW], b_er.rearrange("a g e -> a (g e)").to_broadcast([P, NE]))\
                        .then_inc(ld_router, 16)
                if p == 3:
                    sp.wait_ge(S["g_ready"], 1)
                    sp.dma_start(bias_dram, spread(gdist[:], 1, P)).then_inc(st_bias, 16)
                if p == 5:
                    sp.wait_ge(st_bias, 16)
                    sp.wait_ge(S["xt_mm"], 2 * TB)
                    sp.dma_start(bias, bass.AP(bias_dram.tensor, P - 1, [[640 - 1, P], [P * 640, H], [1, T]]))\
                        .then_inc(ld_bias, 16)
            sp.wait_ge(S["w_lo"], NPROJ)
            sp.dma_start(wao, w_attn_out[0].rearrange("(k p) n -> p k n", p=P)).then_inc(ld_wao, 16)
            sp.wait_ge(S["unit_mm"], NPROJ)
            sp.dma_start(wco, w_conv_out[0].rearrange("(k p) n -> p k n", p=P)).then_inc(ld_wco, 16)
            wo_in = w_out[0].rearrange("(k p) n -> p k n", p=P)
            for hf, before_ in ((0, CO0), (1, WO0)):
                sp.wait_ge(S["w_lo"], before_)
                sp.dma_start(wout[hf], wo_in[:, :, hf * BANK:(hf + 1) * BANK]).then_inc(ld_wout[hf], 16)
            sp.wait_ge(S["o_lo"], CC)
            sp.dma_start(g_bc[:, 0, :], g_ffn.to_broadcast([P, D])).then_inc(ld_gbc, 16)
            sp.dma_start(g_bc[:, 1, :], g_final.rearrange("(a n) -> a n", a=1).to_broadcast([P, D]))\
                .then_inc(ld_gbc, 16)

            def load_expert(slot, pair, e, half):
                ks = slice(KD // 2 * half, KD // 2 * (half + 1))
                for m, w in enumerate((w_e_gate, w_e_up)):
                    sp.dma_start(w_gu[slot][:, e, m, ks, :],
                                 w[0, bass.ds(pair * 2 + e, 1)].rearrange("a (p k) f -> p (a k) f", k=KD)[:, ks, :])\
                        .then_inc(ld_gu[slot], 16)

            def load_half(slot, pair, half):
                for e in range(2):
                    load_expert(slot, pair, e, half)

            def load_down(slot, pair):
                for e in range(2):
                    ex = pair * 2 + e
                    sp.dma_start(w_dn[slot][:, e, :, :],
                                 w_e_down[0, bass.ds(ex, 1)].rearrange("a (p j) n -> p (a j) n", j=2))\
                        .then_inc(ld_dn[slot], 16)

            sp.wait_ge(S["w_lo"], NUNIT)
            load_down(0, 0)
            for half in range(2):
                load_expert(0, 0, 0, half)
            sp.wait_ge(S["wo_mm"], TB)
            for half in range(2):
                load_expert(0, 0, 1, half)
            for b in range(TB):
                sp.wait_ge(S["h2_ready"], b + 1)
                sp.dma_start(h2_dram[b * P:(b + 1) * P, :], h2row[:, b, :]).then_inc(st_h2, 16)
            for half in range(2):
                load_half(1, 1, half)
            load_down(1, 1)
            sp.wait_ge(S["tab_ready"], 1)
            with sp.Fori(1, PAIRS // 2) as i:
                for slot in range(2):
                    used = sp.value_load(tab[0:1, bass.ds(2 * i - 1 + slot, 1)], min_val=1, max_val=MAXT)
                    sp.wait_ge(S["gu_half"], used)
                    load_half(slot, 2 * i + slot, 0)
                    sp.wait_ge(S["gu_mm"], used)
                    load_half(slot, 2 * i + slot, 1)
                    sp.wait_ge(S["y_mm"], 2 * used)
                    load_down(slot, 2 * i + slot)
            tiles = sp.value_load(tab[0:1, PAIRS:PAIRS + 1], min_val=PAIRS, max_val=MAXT - 1)
            for n in range(RING):
                sp.wait_ge(scattered[n], ((tiles + (RING - 1 - n)) // RING) * 16)
            for b in range(TB):
                if b == 2:
                    sp.wait_ge(S["xtev_a"], tiles + 1)
                    sp.wait_ge(S["xtev_v"], tiles + 1)
                for c in range(2):
                    sp.dma_start(yrow[:, 2 * ((b + 2) % TB) + c, :], y_dram[c * T + b * P:c * T + (b + 1) * P, :])\
                        .then_inc(ld_y[b], 16)
            for b in range(TB):
                sp.wait_ge(S["o_ready"], b + 1)
                if b < TB - 1:
                    sp.wait_ge(S["o_half"], b + 1)
                sp.dma_start(out[0, b * P:(b + 1) * P, :], xr[:, b, :]).then_inc(st_out, 16)
            sp.wait_ge(st_out, 16 * TB)

        @block.gpsimd
        def _(pool):
            g = nc.gpsimd
            done = [0]

            def link(ins):
                done[0] += 1
                ins.then_inc(S["pool_chain"], 1)
                pool.wait_ge(S["pool_chain"], done[0])

            for name in ("hid_ready", "hidT_mm", "hidT_ev", "yev_a", "yev_v") + ("ys_free",) * RING:
                pool.sem_inc(S[name], 1)
            g.memset(mhalf[:], -0.5)
            link(g.memset(ident[:], 0.0))
            link(g.affine_select(out=ident[:], in_=ident[:], compare_op=ALU.not_equal, fill=1.0, base=0,
                                 pattern=[[-1, P]], channel_multiplier=1))
            g.memset(ones[:], 1.0)
            for c in range(CC):
                g.memset(glu[:, c, 0:PAD], 0.0)
            g.memset(gdist[:], 0.0)
            g.memset(ones_b[:], 1.0).then_inc(S["consts_ready"], 1)
            pool.wait_ge(S["consts_ready"], 1)
            for b in range(TB):
                pool.wait_ge(S["var_ready"], b + 1)
                g.tensor_tensor(rs[:, 0, b:b + 1], ss[:, 0, b:b + 1], mhalf[:], ALU.pow)\
                    .then_inc(S["rstd_ready"], 1)
            g.affine_select(out=before[:], in_=ones_b[:], compare_op=ALU.is_gt, fill=0.0, base=0,
                            pattern=[[1, P]], channel_multiplier=-1)
            g.iota(iota64[:], pattern=[[1, 64]], base=0, channel_multiplier=0, allow_small_or_imprecise_dtypes=True)
            g.iota(part1[:], pattern=[[1, 1]], base=1, channel_multiplier=1, allow_small_or_imprecise_dtypes=True)
            g.iota(blkcode[:], pattern=[[T, 2], [P, TB]], base=0, channel_multiplier=0,
                   allow_small_or_imprecise_dtypes=True)
            g.iota(half32[:], pattern=[[0, PAIRS], [32, 2]], base=0, channel_multiplier=0,
                   allow_small_or_imprecise_dtypes=True)
            g.iota(rev[:], pattern=[[-1, EG]], base=EG, channel_multiplier=0, allow_small_or_imprecise_dtypes=True)
            link(g.memset(mask[:, 0:P], 0.0))
            g.memset(mask[0:CHUNK, CHUNK:P], MASKED).then_inc(S["consts_ready"], 1)

            def split_lo(u):
                pool.wait_ge(S["w_hi"], u + 1)
                g.tensor_tensor(unit_part(u, 1), unit_raw(u), unit_part(u, 0).bitcast(F32), ALU.subtract)\
                    .then_inc(S["w_lo"], 1)

            def bias_mask(i):
                b, gr = attn[i]
                n = P * (b + 1)
                if i == 0:
                    pool.wait_ge(ld_bias, 16)
                    pool.wait_ge(S["consts_ready"], 2)
                    pool.wait_ge(S["mask_ready"], TB - 1)
                else:
                    pool.wait_ge(S["lg_done"], 4 * i)
                for r in range(4):
                    g.tensor_tensor(bm[:, r, 0:n], bias[:, 4 * gr + r, T - n:T], mask[:, MOFF[b]:MOFF[b] + n],
                                    ALU.add).then_inc(S["bm_ready"], 1)

            for u in range(FREE0):
                split_lo(u)
            bias_mask(0)
            split_lo(FREE0)
            split_lo(FREE0 + 1)
            for i in range(len(attn)):
                if i + 1 < len(attn):
                    bias_mask(i + 1)
                split_lo(units_a[i] + 2)
                if units_b[i]:
                    split_lo(units_b[i] + 2)
            for u in range(NPROJ + 2, NUNIT):
                split_lo(u)
            for b in range(TB):
                pool.wait_ge(S["var_ready"], TB + b + 1)
                g.tensor_tensor(rs[:, 1, b:b + 1], ss[:, 1, b:b + 1], mhalf[:], ALU.pow)\
                    .then_inc(S["rstd_ready"], 1)
            pool.wait_ge(st_h2, 16 * TB)
            pool.wait_ge(S["x2_mm"], 2 * TB)
            pool.wait_ge(S["tab_ready"], 1)

            def hold(n, free=None):
                ins = g.tensor_tensor(carrier[:, n:n + 1], mhalf[:], mhalf[:], ALU.add)
                if free is not None:
                    ins.then_inc(free, 1)

            last_token = pool.to_reg(T - 1)
            last_row = pool.to_reg(2 * T - 1)
            tiles = pool.value_load(tab[0:1, PAIRS:PAIRS + 1], min_val=PAIRS, max_val=MAXT - 1)
            pool.wait_ge(S["tab_ready"], 2)

            def gather(t, u):
                g.tensor_copy(gi1[:, u:u + 1], gidx[:, bass.ds(t, 1)] if not isinstance(t, int) else gidx[:, t:t + 1])\
                    .then_inc(S["idx_copy"], 1)
                pool.wait_ge(S["idx_copy"], t + 1)
                hold(0)
                g.indirect_dma_start(out=ring[:, u, :], out_offset=None, in_=h2_dram,
                                     in_offset=bass.IndirectOffsetOnAxis(ap=gi1[:, u:u + 1], axis=0),
                                     bounds_check=last_token, oob_is_err=False).then_inc(gathered[u], 16)

            gather(0, 0)
            gather(1, 1)
            pool.wait_ge(gathered[0], 16)
            hold(2, S["rows_ready"])
            gather(2, 2)
            gather(3, 3)
            pool.wait_ge(gathered[1], 16)
            hold(3, S["rows_ready"])
            pool.wait_ge(S["xg_ready"], 1)
            gather(RING, 0)
            with pool.Fori(0, MAXT // RING) as i:
                for q in range(RING):
                    t = RING * i + q
                    with pool.If(t < tiles):
                        two_on = (q + 2) % RING
                        pool.wait_ge(gathered[two_on], 16 * i + (16 if q < 2 else 32))
                        hold(3, S["rows_ready"])
                        pool.wait_ge(S["xg_ready"], t + 2)
                        hold(4)
                        gather(t + (RING + 1), (q + 1) % RING)
                        if q == RING - 1:
                            pool.wait_ge(scattered[0], 16 * i + 16)
                            hold(2, S["ys_free"])
                        else:
                            with pool.If(i > 0):
                                pool.wait_ge(scattered[q + 1], 16 * i)
                                hold(2, S["ys_free"])
                        hold(1)
                        g.tensor_copy(si1[:, q:q + 1], sidx[:, bass.ds(t, 1)]).then_inc(S["sidx_copy"], 1)
                        pool.wait_ge(S["sidx_copy"], t + 1)
                        pool.wait_ge(S["yev_a"], t + 2)
                        pool.wait_ge(S["yev_v"], t + 2)
                        hold(5)
                        g.indirect_dma_start(out=y_dram,
                                             out_offset=bass.IndirectOffsetOnAxis(ap=si1[:, q:q + 1], axis=0),
                                             in_=ys[:, q, :], in_offset=None,
                                             bounds_check=last_row, oob_is_err=False).then_inc(scattered[q], 16)
            for b in range(TB):
                pool.wait_ge(S["var_ready"], 2 * TB + b + 1)
                g.tensor_tensor(rs[:, 2, b:b + 1], ss[:, 2, b:b + 1], mhalf[:], ALU.pow)\
                    .then_inc(S["rstd_ready"], 1)
                if b:
                    pool.wait_ge(S["o_scaled"], b)
                    g.tensor_tensor(xr[:, b - 1, BANK:D], xr[:, b - 1, BANK:D], g_bc[:, 1, BANK:D], ALU.mult)\
                        .then_inc(S["o_half"], 1)

        @block.tensor
        def _(pe):
            mm = nc.tensor.matmul
            tr = nc.tensor.transpose
            pe.wait_ge(S["consts_ready"], 1)
            def transpose_rows(rows, ready, mm_sem, ev_sem, banks, after=None):
                for b in range(TB):
                    pe.wait_ge(ready, b + 1)
                    view = rows[:, b, :].rearrange("p (q k) -> p k q", k=KD)
                    for kh in range(2):
                        n = 2 * b + kh
                        if n >= len(banks):
                            pe.wait_ge(ev_sem, n - len(banks) + 1)
                        for kk in range(4):
                            last = tr(bank[banks[n % len(banks)]][:, kk * P:(kk + 1) * P], view[:, 4 * kh + kk, :],
                                      ident[:])
                        last.then_inc(mm_sem, 1)
                    if after and b:
                        after(b - 1)
                if after:
                    after(TB - 1)

            transpose_rows(hrow, S["h_ready"], S["xt_mm"], S["hlo_ready"], (4, 5, 6, 7))
            pe.wait_ge(S["hlo_ready"], 2 * TB)

            def products(out_, a_parts, b_parts, start, stop):
                turns = ((0, 0), (0, 1), (1, 0))
                for x_, (p, q) in enumerate(turns):
                    last = mm(out_, a_parts[p], b_parts[q], start=start and x_ == 0, stop=stop and x_ == 2)
                return last

            def project(u):
                pe.wait_ge(S["w_lo"], u + 1)
                if u >= 2:
                    pe.wait_ge(S["unit_ev"], u - 1)
                if u in (2, 3, 4):
                    pe.wait_ge(S["index_lo"], u - 1)
                w = [unit_part(u, p) for p in range(2)]
                for k in range(KD):
                    last = products(bank[u % 2][0:w[0].shape[2], :], [w[0][:, k, :], w[1][:, k, :]],
                                    [h_hi[:, k, :], h_lo[:, k, :]], k == 0, k == KD - 1)
                last.then_inc(S["unit_mm"], 1)

            def index_products(group):
                b, hb = 1 + group // 2, group % 2
                n = P * (b + 1)
                for i in range(4):
                    turn = 4 * group + i
                    if turn >= 4:
                        pe.wait_ge(S["ix_relu"], turn - 3)
                    rows = slice(32 * i, 32 * i + 32)
                    products(bank[2 + i][:, 0:n], [qi_part[rows, p, hb, b * P:(b + 1) * P] for p in range(2)],
                             [ki_part[rows, p, 0:n] for p in range(2)], True, True).then_inc(S["ix_mm"], 1)

            for u in range(4):
                project(u)
            for b in range(TB):
                last = tr(bank[7][:, b * IH:(b + 1) * IH], wiT[:, b * P:(b + 1) * P], ident[0:IH, 0:IH])
            last.then_inc(S["vt_mm"], 1)
            pe.wait_ge(S["index_lo"], 3)
            index_products(0)
            project(4)
            index_products(1)
            project(5)
            pe.wait_ge(ld_rows, 64)
            pe.wait_ge(S["vt_ev"], 1)
            for c in range(CC):
                last = tr(bank[7][:, c * (TAPS + 3):(c + 1) * (TAPS + 3)], cvrow[:, c * P:(c + 1) * P],
                          ident[0:TAPS + 3, 0:TAPS + 3])
            last.then_inc(S["cv_mm"], 1)
            pe.wait_ge(S["unit_ev"], 5)
            for b in range(TB):
                last = tr(bank[6][:, b * P:(b + 1) * P], vT[:, b * P:(b + 1) * P], ident[:])
            last.then_inc(S["vt_mm"], 1)
            for group, units in ((2, (6,)), (3, (7, 8)), (4, (9,)), (5, range(10, FREE0 - 2))):
                index_products(group)
                for u in units:
                    project(u)

            def logits(i):
                b, gr = attn[i]
                n = P * (b + 1)
                for r in range(4):
                    h = 4 * gr + r
                    lo = HEAD_DIM * (h % 2)
                    if i:
                        pe.wait_ge(S["lg_done"], 4 * (i - 1) + r + 1)
                    mm(bank[2 + r][:, 0:n], qT[lo:lo + HEAD_DIM, h // 2, b * P:(b + 1) * P],
                       kT[lo:lo + HEAD_DIM, gr, 0:n], start=True, stop=True).then_inc(S["qk_mm"], 1)

            pe.wait_ge(S["ix_relu"], 24)
            pe.wait_ge(S["vt_ev"], 2)
            logits(0)
            project(FREE0 - 2)
            project(FREE0 - 1)
            for i, (b, gr) in enumerate(attn):
                if i + 1 < len(attn):
                    logits(i + 1)
                project(units_a[i])
                pe.wait_ge(S["unit_ev"], units_a[i])
                pe.wait_ge(S["p_ready"], i + 1)
                for s in range(b + 1):
                    if s >= 2:
                        pe.wait_ge(S["pt_ev"], tiles_before[i] + s - 1)
                    to = bank[pt_bank(i, s)]
                    for r in range(4):
                        last = tr(to[:, r * P:(r + 1) * P], prob[i % 2][:, r, s * P:(s + 1) * P], ident[:])
                    last.then_inc(S["pt_mm"], 1)
                pe.wait_ge(S["pt_ev"], tiles_before[i + 1])
                if i:
                    pe.wait_ge(S["ot_ev"], i)
                for s in range(b + 1):
                    for par in range(2):
                        lo = HEAD_DIM * par
                        last = mm(bank[7][lo:lo + HEAD_DIM, 0:2 * P],
                                  vrow[:, s, gr * HEAD_DIM:(gr + 1) * HEAD_DIM], pT[:, s, par::2, :],
                                  start=(s == 0), stop=(s == b))
                last.then_inc(S["pv_mm"], 1)
                if i == len(attn) - 1:
                    pe.wait_ge(S["conv_ready"], 1)
                    for c in range(CC):
                        last = mm(bank[6][:], ones[:], yv[:, c, :], start=(c == 0), stop=(c == CC - 1))
                    last.then_inc(S["ln_mm"], 1)
                if units_b[i]:
                    project(units_b[i])
            pe.wait_ge(S["ot_ev"], len(attn))
            for c in range(CC):
                pe.wait_ge(S["sq_ready"], c + 1)
                last = mm(bank[7][:], ones[:], sT[:, c, :], start=(c == 0), stop=(c == CC - 1))
            last.then_inc(S["ln_mm"], 1)
            pe.wait_ge(S["lg_done"], 4 * len(attn))

            def branch_out(u, parts):
                pe.wait_ge(S["w_lo"], u + 1)
                turn = u - AO0
                if turn >= 4:
                    pe.wait_ge(S["branch_ev"], turn - 3)
                w = [unit_part(u, p) for p in range(2)]
                for c in range(CC):
                    last = products(bank[2 + u % 4][:], [w[0][:, c, :], w[1][:, c, :]],
                                    [parts[:, 0, c, :], parts[:, 1, c, :]], c == 0, c == CC - 1)
                last.then_inc(S["unit_mm"], 1)

            pe.wait_ge(S["o_lo"], CC)
            for u in range(AO0, CO0):
                branch_out(u, o_part)
            pe.wait_ge(S["s_lo"], CC)
            for u in range(CO0, WO0):
                branch_out(u, s_part)
            def merged_products(hf, b, u, kk):
                k = 2 * (u - WO0) % KD + kk
                return products(bank[wo_bank(hf, b)][:],
                                [m_hi[:, k, b * P:(b + 1) * P], m_lo[:, k, b * P:(b + 1) * P]],
                                [unit_part(u, p)[:, kk, :] for p in range(2)], k == 0, k == KD - 1)

            pe.wait_ge(S["unit_ev"], NPROJ)
            for u in range(WO0, WO1):
                pe.wait_ge(S["w_lo"], u + 1)
                pe.wait_ge(S["m_lo"], 2 * (u - WO0) + 2)
                for b in range(TB):
                    for kk in range(2):
                        last = merged_products(0, b, u, kk)
                last.then_inc(S["unit_mm"], 1)
            pe.wait_ge(S["branch_ev"], 2 * KD)
            for b in range(TB):
                for u in range(WO1, NUNIT):
                    if b == 0:
                        pe.wait_ge(S["w_lo"], u + 1)
                    for kk in range(2):
                        last = merged_products(1, b, u, kk)
                last.then_inc(S["wo_mm"], 1)

            def router_logits(b):
                pe.wait_ge(S["x2_ev"], 2 * b + 2)
                for k in range(KD):
                    last = mm(bank[1][:, b * LW:(b + 1) * LW], h2T[:, k, b * P:(b + 1) * P], wr[:, k, :],
                              start=(k == 0), stop=(k == KD - 1))
                if b == TB - 1:
                    last.then_inc(S["rt_mm"], 1)

            pe.wait_ge(S["wr_ready"], 1)
            pe.wait_ge(S["wo_ev"], TB)
            transpose_rows(h2row, S["h2_ready"], S["x2_mm"], S["x2_ev"], (6, 7), router_logits)
            pe.wait_ge(S["m_ready"], 1)
            pe.wait_ge(S["wo_ev"], 2 * TB)
            flat = lambda a: a[:, :, :].rearrange("p b e -> p (b e)")
            mm(bank[2][:, 0:TB * NE], before[:], flat(Mb), start=True, stop=False)
            mm(bank[2][:, 0:TB * NE], ones_b[:], flat(Mpre), start=False, stop=True)
            mm(bank[3][:, 0:NE], ones_b[:], Mtot, start=True, stop=True).then_inc(S["rank_mm"], 1)
            pe.wait_ge(S["oh_ready"], 1)
            for cc in range(2 * TB):
                for hf in range(2):
                    last = mm(bank[4][64 * hf:64 * hf + 64, 0:2 * MAXT], ohlo[:, cc, :],
                              ohv[:, cc, :, hf * MAXT:(hf + 1) * MAXT], start=(cc == 0), stop=(cc == 2 * TB - 1))
            last.then_inc(S["tab_mm"], 1)

            def transpose_tile(t):
                pe.wait_ge(S["xg_ready"], t + 1)
                view = xg.rearrange("p (q k) -> p k q", k=KD)
                for kh in range(2):
                    for kk in range(4):
                        last = tr(bank[6 + kh][:, kk * P:(kk + 1) * P], view[:, 4 * kh + kk, :], ident[:])
                    last.then_inc(S["xg_mm"], 1)

            pe.wait_ge(S["x2_ev"], 2 * TB)
            transpose_tile(0)
            with pe.Fori(0, PAIRS // 2) as i:
                for slot in range(2):
                    first = pe.value_load(tab[0:1, bass.ds(2 * i + slot, 1)], min_val=0, max_val=MAXT - 1)
                    end = pe.value_load(tab[0:1, bass.ds(2 * i + (slot + 1), 1)], min_val=1, max_val=MAXT - 1)
                    with pe.Fori(first, end) as t:
                        pe.wait_ge(ld_gu[slot], 128 * i + 128)
                        pe.wait_ge(S["xtev_a"], t + 1)
                        pe.wait_ge(S["xtev_v"], t + 1)
                        pe.wait_ge(S["hid_ready"], t + 1)
                        for k in range(KD):
                            for e in range(2):
                                last = mm(bank[0][64 * e:64 * e + 64, :], xTs[:, k, 64 * e:64 * e + 64],
                                          w_gu[slot][:, e, :, k, :], start=(k == 0), stop=(k == KD - 1))
                            if k == KD // 2 - 1:
                                last.then_inc(S["gu_half"], 1)
                        last.then_inc(S["gu_mm"], 1)
                        transpose_tile(t + 1)
                        pe.wait_ge(S["hid_ready"], t + 2)
                        pe.wait_ge(S["hidT_ev"], t + 1)
                        view = hid.rearrange("p (q j) -> p j q", j=2)
                        for j in range(2):
                            last = tr(bank[1][:, j * P:(j + 1) * P], view[:, j, :], ident[:])
                        last.then_inc(S["hidT_mm"], 1)
                        pe.wait_ge(S["hidT_ev"], t + 2)
                        pe.wait_ge(S["yev_a"], t + 1)
                        pe.wait_ge(S["yev_v"], t + 1)
                        pe.wait_ge(ld_dn[slot], 32 * i + 32)
                        for n in range(2):
                            for j in range(2):
                                for e in range(2):
                                    last = mm(bank[2 + n][64 * e:64 * e + 64, :], hidT[:, j, 64 * e:64 * e + 64],
                                              w_dn[slot][:, e, j, n * BANK:(n + 1) * BANK],
                                              start=(j == 0), stop=(j == 1))
                            last.then_inc(S["y_mm"], 1)

        @block.scalar
        def _(act):
            a = nc.scalar.activation
            act.dma_start(gmix, g_mix.to_broadcast([P, D])).then_inc(ld_gmix, 16)

            def split_hi(u):
                if u == 0:
                    act.wait_ge(ld_small, 16)
                elif u < AO0:
                    p = (u - 1) // 2
                    act.wait_ge(ld_win[p % 2], 16 * (p // 2) + 16)
                elif u < CO0:
                    act.wait_ge(ld_wao, 16)
                elif u < WO0:
                    act.wait_ge(ld_wco, 16)
                else:
                    act.wait_ge(ld_wout[(u - WO0) // 4], 16)
                if u >= WO1:
                    act.wait_ge(S["unit_mm"], CO0 if u < WO1 + 2 else WO0)
                elif u >= 2:
                    act.wait_ge(S["unit_mm"], u - 1)
                a(unit_part(u, 0), unit_raw(u), ACT.Copy).then_inc(S["w_hi"], 1)

            def unit_out(u):
                act.wait_ge(S["unit_mm"], u + 1)
                src = bank[u % 2]
                if u == 0:
                    for i in range(4):
                        a(ki_part[32 * i:32 * i + 32, 0, :], src[0:ID, :], ACT.Copy)
                    last = a(wiT, src[ID:ID + IH, :], ACT.Copy)
                elif u < 3:
                    last = a(qi_part[:, 0, u - 1, :], src[:], ACT.Copy)
                elif u == 3:
                    for gr in range(2):
                        for lo in range(2):
                            last = a(kT[64 * lo:64 * lo + 64, gr, :], src[64 * gr:64 * gr + 64, :], ACT.Copy)
                elif u == 4:
                    last = a(vT, src[:], ACT.Copy)
                elif u < 9:
                    last = a(qT[:, u - 5, :], src[:], ACT.Copy, scale=HEAD_DIM ** -0.5)
                elif u < 13:
                    last = a(glu[:, u - 9, PAD:PAD + T], src[:], ACT.Copy)
                elif u < 17:
                    last = a(sig[:, u - 13, :], src[:], ACT.Sigmoid)
                elif u < 25:
                    last = a(gB[:, u - 17, :], src[:], ACT.Copy)
                else:
                    last = a(gA[:, u - 25, :], src[:], ACT.Copy)
                last.then_inc(S["unit_ev"], 1)

            def step(u):
                split_hi(u + 2)
                unit_out(u)

            def index_relu(group):
                n = P * (2 + group // 2)
                for i in range(4):
                    turn = 4 * group + i
                    act.wait_ge(S["ix_mm"], turn + 1)
                    if turn >= 8:
                        act.wait_ge(S["ix_acc"], turn - 7)
                    a(relu[:, turn % 8, 0:n], bank[2 + i][:, 0:n], ACT.Relu).then_inc(S["ix_relu"], 1)

            for b in range(TB):
                act.wait_ge(ld_x[b], 16)
                a(gflat[:, b * D:(b + 1) * D], xr[:, b, :], ACT.Square, accum_out=ss[:, 0, b:b + 1])\
                    .then_inc(S["ss_done"], 1)
            for n in range(2 * TB):
                if n == 4:
                    split_hi(0)
                    split_hi(1)
                act.wait_ge(S["xt_mm"], n + 1)
                b, kh = n // 2, n % 2
                a(h_hi[:, 4 * kh:4 * kh + 4, b * P:(b + 1) * P],
                  bank[4 + n % 4][:].rearrange("p (k n) -> p k n", k=4), ACT.Copy).then_inc(S["hhi_ready"], 1)
            act.wait_ge(S["ss_done"], TB)
            for u in range(4):
                step(u)
            act.wait_ge(S["vt_mm"], 1)
            a(wi[:, :, :].rearrange("p b h -> p (b h)"), bank[7][:, 0:TB * IH], ACT.Copy,
              scale=float(ID * IH) ** -0.5).then_inc(S["vt_ev"], 1)
            index_relu(0)
            step(4)
            index_relu(1)
            step(5)
            act.wait_ge(S["cv_mm"], 1)
            a(cv[:, :, :].rearrange("p c n -> p (c n)"), bank[7][:, 0:CC * (TAPS + 3)], ACT.Copy)\
                .then_inc(S["cv_ev"], 1)
            act.wait_ge(S["vt_mm"], 2)
            a(vrow[:, :, :].rearrange("p b n -> p (b n)"), bank[6][:], ACT.Copy).then_inc(S["vt_ev"], 1)
            for group, units in ((2, (6,)), (3, (7, 8)), (4, (9,)), (5, range(10, FREE0 - 1))):
                index_relu(group)
                for u in units:
                    step(u)

            def exps(i):
                n = P * (attn[i][0] + 1)
                act.wait_ge(S["nm_ready"], i + 1)
                for r in range(4):
                    last = a(prob[i % 2][:, r, 0:n], prob[i % 2][:, r, 0:n], ACT.Exp, bias=nm[:, i % 2, r:r + 1],
                             accum_out=sm[:, i % 2, r:r + 1])
                last.then_inc(S["ex_done"], 1)

            exps(0)
            step(FREE0 - 1)
            for i, (b, gr) in enumerate(attn):
                n = P * (b + 1)
                act.wait_ge(S["ri_ready"], i + 1)
                for r in range(4):
                    last = a(prob[i % 2][:, r, 0:n], prob[i % 2][:, r, 0:n], ACT.Copy, scale=ri[:, i % 2, r:r + 1])
                last.then_inc(S["p_ready"], 1)
                if i:
                    act.wait_ge(S["pv_mm"], i)
                for s in range(b + 1):
                    act.wait_ge(S["pt_mm"], tiles_before[i] + s + 1)
                    a(pT[:, s, :, :].rearrange("p r n -> p (r n)"), bank[pt_bank(i, s)][:], ACT.Copy)\
                        .then_inc(S["pt_ev"], 1)
                step(units_a[i])
                if i + 1 < len(attn):
                    exps(i + 1)
                else:
                    act.wait_ge(S["pv_mm"], len(attn))
                    for c in range(CC):
                        act.wait_ge(S["yc_ready"], c + 1)
                        a(sT[:, c, :], yv[:, c, :], ACT.Square).then_inc(S["sq_ready"], 1)
                if units_b[i]:
                    step(units_b[i])
            act.wait_ge(S["ot_ev"], len(attn))
            for c in range(CC):
                a(o_part[:, 0, c, :], oT[:, c, :], ACT.Copy).then_inc(S["o_hi"], 1)
            act.wait_ge(S["unit_ev"], NPROJ)

            def gate(chunks):
                a(chunks, chunks, ACT.Sigmoid).then_inc(S["gate_ready"], 1)

            act.wait_ge(S["lnvar_ready"], 1)
            a(work, score, ACT.Sqrt).then_inc(S["lnstd_ready"], 1)
            split_hi(AO0 + 2)
            gate(gB[:, 0:4, :])
            split_hi(AO0 + 3)
            split_hi(AO0 + 4)
            for c in range(CC):
                act.wait_ge(S["z_ready"], c + 1)
                a(sT[:, c, :], yv[:, c, :], ACT.Silu, scale=cv[:, c, TAPS + 1:TAPS + 2],
                  bias=cv[:, c, TAPS + 2:TAPS + 3]).then_inc(S["silu_ready"], 1)
            split_hi(AO0 + 5)
            for c in range(CC):
                act.wait_ge(S["silu_ready"], c + 1)
                a(s_part[:, 0, c, :], sT[:, c, :], ACT.Copy).then_inc(S["s_hi"], 1)
            split_hi(AO0 + 6)
            split_hi(AO0 + 7)
            gate(gB[:, 4:8, :])
            split_hi(CO0)
            split_hi(CO0 + 1)
            gate(gA[:, 0:4, :])
            split_hi(CO0 + 2)
            gate(gA[:, 4:8, :])
            for n in range(KD):
                if n:
                    split_hi(CO0 + 2 + n)
                act.wait_ge(S["merged"], n + 1)
                a(m_hi[:, n, :], gA[:, n, :], ACT.Copy).then_inc(S["m_hi"], 1)
            for u in range(WO0 + 2, NUNIT):
                split_hi(u)
            for b in range(TB):
                act.wait_ge(S["wo_ev"], TB + b + 1)
                a(conv_buf[:, 2 * b:2 * b + 2, :].rearrange("p k n -> p (k n)"), xr[:, b, :], ACT.Square,
                  accum_out=ss[:, 1, b:b + 1]).then_inc(S["ss_done"], 1)
            act.wait_ge(S["ss_done"], 2 * TB)
            for n in range(2 * TB):
                act.wait_ge(S["x2_mm"], n + 1)
                b, kh = n // 2, n % 2
                a(h2T[:, 4 * kh:4 * kh + 4, b * P:(b + 1) * P],
                  bank[6 + n % 2][:].rearrange("p (k n) -> p k n", k=4), ACT.Copy).then_inc(S["x2_ev"], 1)
            act.wait_ge(S["exp_in"], 1)
            a(gw[:, 1, :, 0:NG], gw[:, 0, :, 0:NG], ACT.Exp).then_inc(S["exp_out"], 1)
            act.wait_ge(S["exp_in"], 2)
            a(gs[:, 8, :], gs[:, 7, :], ACT.Exp).then_inc(S["exp_out"], 1)
            act.wait_ge(S["tab_ready"], 1)

            def rows_T(t):
                act.wait_ge(S["xg_mm"], 2 * t + 1)
                a(xTs[:, 0:4, :].rearrange("p k n -> p (k n)"), bank[6][:], ACT.Copy).then_inc(S["xtev_a"], 1)

            tiles = act.value_load(tab[0:1, PAIRS:PAIRS + 1], min_val=PAIRS, max_val=MAXT - 1)
            rows_T(0)
            with act.Fori(0, tiles) as t:
                act.wait_ge(S["gu_mm"], t + 1)
                act.wait_ge(S["hid_ready"], t + 1)
                a(sil, bank[0][:, 0:FF], ACT.Silu).then_inc(S["silu_g"], 1)
                rows_T(t + 1)
                act.wait_ge(S["y_mm"], 2 * t + 2)
                act.wait_ge(S["ys_free"], t + 1)
                a(ys[:, t % RING, BANK:2 * BANK], bank[3][:], ACT.Copy).then_inc(S["yev_a"], 1)
            for b in range(TB):
                act.wait_ge(S["y_add"], 2 * b + 2)
                a(conv_buf[:, 2 * b:2 * b + 2, :].rearrange("p k n -> p (k n)"), xr[:, b, :], ACT.Square,
                  accum_out=ss[:, 2, b:b + 1]).then_inc(S["ss_done"], 1)
                if b:
                    act.wait_ge(S["rstd_ready"], 2 * TB + b)
                    a(xr[:, b - 1, BANK:D], xr[:, b - 1, BANK:D], ACT.Copy, scale=rs[:, 2, b - 1:b])\
                        .then_inc(S["o_scaled"], 1)

        @block.vector
        def _(dve):
            v = nc.vector
            done = [0]

            def link(ins):
                done[0] += 1
                ins.then_inc(S["dve_chain"], 1)
                dve.wait_ge(S["dve_chain"], done[0])

            def mean_square(which, b):
                dve.wait_ge(S["ss_done"], TB * which + b + 1)
                v.tensor_scalar(ss[:, which, b:b + 1], ss[:, which, b:b + 1], 1.0 / D, EPS, ALU.mult, ALU.add)\
                    .then_inc(S["var_ready"], 1)

            dve.wait_ge(ld_gmix, 16)

            def h_low(n):
                dve.wait_ge(S["hhi_ready"], n + 1)
                b, kh = n // 2, n % 2
                at_ = (slice(None), slice(4 * kh, 4 * kh + 4), slice(b * P, (b + 1) * P))
                v.tensor_tensor(h_lo[at_], bank[4 + n % 4][:].rearrange("p (k n) -> p k n", k=4),
                                h_hi[at_].bitcast(F32), ALU.subtract).then_inc(S["hlo_ready"], 1)

            mean_square(0, 0)
            for b in range(TB):
                if b + 1 < TB:
                    mean_square(0, b + 1)
                dve.wait_ge(S["rstd_ready"], b + 1)
                v.scalar_tensor_tensor(hrow[:, b, :], xr[:, b, :], rs[:, 0, b:b + 1], gmix, ALU.mult, ALU.mult)\
                    .then_inc(S["h_ready"], 1)
                if b >= 2:
                    h_low(2 * b - 4)
                    h_low(2 * b - 3)
            for n in range(2 * TB - 4, 2 * TB):
                h_low(n)
            dve.wait_ge(ld_relb, 16)
            dve.wait_ge(S["consts_ready"], 1)
            for lo, hi_, k in bucket_runs(-(P - 1), T - 1):
                last = v.tensor_copy(gdist[:, T - 1 - hi_:T - lo], relbT[:, k:k + 1].to_broadcast([H, hi_ - lo + 1]))
            last.then_inc(S["g_ready"], 1)
            dve.wait_ge(S["unit_ev"], 1)
            for i in range(4):
                last = v.tensor_tensor(ki_part[32 * i:32 * i + 32, 1, :], bank[0][0:ID, :],
                                       ki_part[0:ID, 0, :].bitcast(F32), ALU.subtract)
            last.then_inc(S["index_lo"], 1)
            for j in range(2):
                dve.wait_ge(S["unit_ev"], 2 + j)
                v.tensor_tensor(qi_part[:, 1, j, :], bank[1 - j][:], qi_part[:, 0, j, :].bitcast(F32), ALU.subtract)\
                    .then_inc(S["index_lo"], 1)
            dve.wait_ge(S["vt_ev"], 1)
            for b in range(1, TB):
                n = P * (b + 1)
                for h in range(IH):
                    turn = (b - 1) * IH + h
                    dve.wait_ge(S["ix_relu"], turn + 1)
                    w = wi[:, b, h:h + 1]
                    if h == 0:
                        ins = v.tensor_scalar(index_score[:, 0:n], relu[:, turn % 8, 0:n], w, None, ALU.mult)
                    else:
                        ins = v.scalar_tensor_tensor(index_score[:, 0:n], relu[:, turn % 8, 0:n], w,
                                                     index_score[:, 0:n], ALU.mult, ALU.add)
                    ins.then_inc(S["ix_acc"], 1)
                    dve.wait_ge(S["ix_acc"], turn + 1)
                link(v.memset(index_score[0:CHUNK, n - CHUNK:n], NEG))
                src = index_score
                for _ in range(TOPK // 8):
                    link(v.max(m8[:], src[:, 0:n]))
                    link(v.match_replace(work[:, 0:n], m8[:], src[:, 0:n], NEG))
                    src = work
                link(v.tensor_tensor(work[:, 0:n], work[:, 0:n], index_score[:, 0:n], ALU.is_equal))
                v.tensor_scalar(mask[:, MOFF[b]:MOFF[b] + n], work[:, 0:n], MASKED, None, ALU.mult)\
                    .then_inc(S["mask_ready"], 1)
            for c in range(CC):
                dve.wait_ge(S["unit_ev"], 14 + c)
                v.tensor_tensor(glu[:, c, PAD:PAD + T], glu[:, c, PAD:PAD + T], sig[:, c, :], ALU.mult)\
                    .then_inc(S["glu_done"], 1)
            dve.wait_ge(S["glu_done"], CC)
            dve.wait_ge(S["cv_ev"], 1)

            TAPU = 3
            TURNS = (TAPS - 1) // TAPU
            turns_done = [0]

            def conv_piece(turns):
                pair, first = divmod(turns_done[0], TURNS)
                turns_done[0] += turns
                blocks = (2 * pair, 2 * pair + 1)
                base = pair * 2 * TAPS
                if first == 0:
                    for c in blocks:
                        v.tensor_scalar(yv[:, c, :], glu[:, c, 0:T], cv[:, c, 0:1], cv[:, c, TAPS:TAPS + 1],
                                        ALU.mult, ALU.add).then_inc(S["conv_step"], 1)
                with dve.Fori(0, turns) as i:
                    for u in range(TAPU):
                        for c in blocks:
                            dve.wait_ge(S["conv_step"], i * (2 * TAPU)
                                        + (base + first * 2 * TAPU + 2 * u + (c - blocks[0]) + 1))
                            v.scalar_tensor_tensor(yv[:, c, :], glu[:, c, bass.ds(i * TAPU + (first * TAPU + u + 1), T)],
                                                   cv[:, c, bass.ds(i * TAPU + (first * TAPU + u + 1), 1)],
                                                   yv[:, c, :], ALU.mult, ALU.add).then_inc(S["conv_step"], 1)

            def logits_out(i):
                n = P * (attn[i][0] + 1)
                if i >= 2:
                    dve.wait_ge(S["pt_mm"], tiles_before[i - 1])
                for r in range(4):
                    dve.wait_ge(S["qk_mm"], 4 * i + r + 1)
                    dve.wait_ge(S["bm_ready"], 4 * i + r + 1)
                    v.tensor_tensor_reduce(out=prob[i % 2][:, r, 0:n], in0=bank[2 + r][:, 0:n],
                                           in1=bm[:, r, 0:n], scale=1.0, scalar=NEG, op0=ALU.add, op1=ALU.max,
                                           accum_out=mx[:, i % 2, r:r + 1]).then_inc(S["lg_done"], 1)
                dve.wait_ge(S["lg_done"], 4 * i + 4)
                v.tensor_scalar(nm[:, i % 2, :], mx[:, i % 2, :], -1.0, None, ALU.mult).then_inc(S["nm_ready"], 1)

            def outputs_out(i):
                b, gr = attn[i]
                dve.wait_ge(S["pv_mm"], i + 1)
                v.tensor_copy(oT[:, 2 * gr:2 * gr + 2, b * P:(b + 1) * P],
                              bank[7][:, 0:2 * P].rearrange("p (j n) -> p j n", j=2)).then_inc(S["ot_ev"], 1)

            conv_piece(3)
            logits_out(0)
            for i, (b, gr) in enumerate(attn):
                conv_piece(3 if i == 2 else 2)
                dve.wait_ge(S["ex_done"], i + 1)
                v.reciprocal(ri[:, i % 2, :], sm[:, i % 2, :]).then_inc(S["ri_ready"], 1)
                if i + 1 < len(attn):
                    logits_out(i + 1)
                if i:
                    outputs_out(i - 1)
            dve.wait_ge(S["conv_step"], CC * TAPS)
            v.memset(m8[:], 0.0).then_inc(S["conv_ready"], 1)
            outputs_out(len(attn) - 1)
            dve.wait_ge(S["ln_mm"], 1)
            for c in range(CC):
                v.scalar_tensor_tensor(yv[:, c, :], bank[6][:], -1.0 / C, yv[:, c, :], ALU.mult, ALU.add)\
                    .then_inc(S["yc_ready"], 1)
            for c in range(CC):
                dve.wait_ge(S["o_hi"], c + 1)
                v.tensor_tensor(o_part[:, 1, c, :], oT[:, c, :], o_part[:, 0, c, :].bitcast(F32), ALU.subtract)\
                    .then_inc(S["o_lo"], 1)

            def attn_branch(n):
                dve.wait_ge(S["gate_ready"], 1 + n // 4)
                dve.wait_ge(S["unit_mm"], AO0 + n + 1)
                v.tensor_tensor(gB[:, n, :], gB[:, n, :], bank[2 + (AO0 + n) % 4][:], ALU.mult)\
                    .then_inc(S["branch_ev"], 1)

            dve.wait_ge(S["ln_mm"], 2)
            v.tensor_scalar(score, bank[7][:], 1.0 / C, EPS, ALU.mult, ALU.add).then_inc(S["lnvar_ready"], 1)
            dve.wait_ge(S["lnstd_ready"], 1)
            link(v.reciprocal(work, work))
            link(v.tensor_tensor(score, score, work, ALU.mult))
            link(v.tensor_tensor(score, score, work, ALU.mult))
            link(v.tensor_scalar(score, score, -0.5, 1.5, ALU.mult, ALU.add))
            link(v.tensor_tensor(work, score, work, ALU.mult))
            for c in range(CC):
                v.tensor_tensor(yv[:, c, :], yv[:, c, :], work, ALU.mult).then_inc(S["z_ready"], 1)
            for n in range(4):
                attn_branch(n)
            for c in range(CC):
                dve.wait_ge(S["s_hi"], c + 1)
                v.tensor_tensor(s_part[:, 1, c, :], sT[:, c, :], s_part[:, 0, c, :].bitcast(F32), ALU.subtract)\
                    .then_inc(S["s_lo"], 1)
            for n in range(4, KD):
                attn_branch(n)

            def merged_low(n):
                dve.wait_ge(S["m_hi"], n + 1)
                v.tensor_tensor(m_lo[:, n, :], gA[:, n, :], m_hi[:, n, :].bitcast(F32), ALU.subtract)\
                    .then_inc(S["m_lo"], 1)

            for n in range(KD):
                dve.wait_ge(S["gate_ready"], 3 + n // 4)
                dve.wait_ge(S["unit_mm"], CO0 + n + 1)
                v.tensor_tensor(gA[:, n, :], gA[:, n, :], bank[2 + (CO0 + n) % 4][:], ALU.mult)\
                    .then_inc(S["branch_ev"], 1)
                dve.wait_ge(S["branch_ev"], KD + n + 1)
                v.tensor_tensor(gA[:, n, :], gA[:, n, :], gB[:, n, :], ALU.add).then_inc(S["merged"], 1)
                if n:
                    merged_low(n - 1)
            merged_low(KD - 1)
            dve.wait_ge(ld_router, 64)
            v.tensor_copy(wr[:, :, 0:NG], wr_g[:])
            for gr in range(NG):
                last = v.tensor_copy(wr[:, :, NG + gr * EG:NG + (gr + 1) * EG], wr_e[:, gr, :, :])
            last.then_inc(S["wr_ready"], 1)
            dve.wait_ge(ld_gbc, 32)

            def residual(hf, b):
                v.tensor_tensor(xr[:, b, hf * BANK:(hf + 1) * BANK], xr[:, b, hf * BANK:(hf + 1) * BANK],
                                bank[wo_bank(hf, b)][:], ALU.add).then_inc(S["wo_ev"], 1)

            dve.wait_ge(S["unit_mm"], WO0 + 4)
            for b in range(TB):
                residual(0, b)
            for b in range(TB):
                dve.wait_ge(S["wo_mm"], b + 1)
                residual(1, b)
                mean_square(1, b)
                dve.wait_ge(S["rstd_ready"], TB + b + 1)
                v.scalar_tensor_tensor(h2row[:, b, :], xr[:, b, :], rs[:, 1, b:b + 1], g_bc[:, 0, :],
                                       ALU.mult, ALU.mult).then_inc(S["h2_ready"], 1)
            dve.wait_ge(S["rt_mm"], 1)
            link(v.tensor_tensor(lg, bank[1][:, 0:TB * LW].rearrange("p (b n) -> p b n", b=TB),
                                 spread(br[:], 1, TB), ALU.add))
            dve.wait_ge(S["consts_ready"], 2)

            def first_max(val, d, mxo, eqw, one, n):
                link(v.tensor_reduce(mxo, val, AX, ALU.max))
                link(v.tensor_tensor(d, val, spread(mxo, 2, n), ALU.subtract))
                link(v.scalar_tensor_tensor(eqw, d, 0.0, spread(rev[:, EG - n:EG], 1, TB), ALU.is_equal, ALU.mult))
                link(v.tensor_reduce(gs[:, 0, :], eqw, AX, ALU.max))
                link(v.tensor_tensor(one, eqw, spread(gs[:, 0, :], 2, n), ALU.is_equal))

            first_max(lg[:, :, 0:NG], gw[:, 0, :, 0:NG], gs[:, 1, :], gw[:, 2, :, 0:NG], gw[:, 3, :, 0:NG], NG)
            v.memset(gs[:, 15, :], 0.0).then_inc(S["exp_in"], 1)
            oneg = gw[:, 3, :, 0:NG]
            link(v.tensor_tensor(e4, lg[:, :, NG:LW].rearrange("p b (g e) -> p b g e", g=NG),
                                 spread(oneg, 3, EG), ALU.mult))
            link(v.tensor_reduce(gw[:, 4, :, :], e4[:, :, :, :].rearrange("p b g e -> p b e g"), AX, ALU.add))
            first_max(gw[:, 4, :, :], gw[:, 5, :, :], gs[:, 2, :], gw[:, 6, :, :], gw[:, 7, :, :], EG)
            link(v.scalar_tensor_tensor(gw[:, 8, :, :], gw[:, 7, :, :], NEG, gw[:, 4, :, :], ALU.mult, ALU.add))
            first_max(gw[:, 8, :, :], gw[:, 9, :, :], gs[:, 3, :], gw[:, 10, :, :], gw[:, 11, :, :], EG)
            v.tensor_tensor(gs[:, 7, :], gs[:, 3, :], gs[:, 2, :], ALU.subtract).then_inc(S["exp_in"], 1)
            for c, one in enumerate((gw[:, 7, :, :], gw[:, 11, :, :])):
                last = v.tensor_tensor(Mf[:, c, :, :].rearrange("p b (g e) -> p b g e", g=NG),
                                       spread(oneg, 3, EG), spread(one, 2, NG), ALU.mult)
            link(last)
            link(v.tensor_tensor(Mb, Mf[:, 0, :, :], Mf[:, 1, :, :], ALU.add))
            link(v.memset(Mpre[:, 0, :], 0.0))
            for b in range(1, TB):
                link(v.tensor_tensor(Mpre[:, b, :], Mpre[:, b - 1, :], Mb[:, b - 1, :], ALU.add))
            v.tensor_tensor(Mtot, Mpre[:, TB - 1, :], Mb[:, TB - 1, :], ALU.add).then_inc(S["m_ready"], 1)
            dve.wait_ge(S["rank_mm"], 1)
            link(v.tensor_scalar(cnti[:], bank[3][:, 0:NE], float(SLOTS - 1), None, ALU.add))
            link(v.tensor_scalar(cnti[:], cnti[:], 6, None, ALU.arith_shift_right))
            link(v.tensor_copy(cnt[:], cnti[:]))
            pairs = cnt[:].rearrange("p (q e) -> p q e", e=2)
            link(v.tensor_reduce(nseg[:], pairs, AX, ALU.max))
            link(v.tensor_scalar(nseg[:], nseg[:], 1.0, None, ALU.max))
            v.memset(tab[:, 0:1], 0)
            link(v.tensor_tensor_scan(tend[:], ones[:, 0:PAIRS], nseg[:], 0.0, ALU.mult, ALU.add))
            v.tensor_copy(tab[:, 1:PAIRS + 1], tend[:]).then_inc(S["tab_ready"], 1)
            link(v.tensor_tensor(nseg[:], tend[:], nseg[:], ALU.subtract))
            link(v.tensor_tensor(hib[:].rearrange("p (q e) -> p q e", e=2), spread(nseg[:], 2, 2),
                                 half32[:].rearrange("p (q e) -> p q e", e=2), ALU.add))
            ranks = bank[2][:, 0:TB * NE].rearrange("p (b e) -> p b e", b=TB)
            for c in range(2):
                v.tensor_tensor(big[:, 0, c, :, :], Mf[:, c, :, :], ranks, ALU.mult)
                last = v.tensor_tensor(big[:, 1, c, :, :], Mf[:, c, :, :], spread(hib[:], 1, TB), ALU.mult)
            link(last)
            v.tensor_reduce(hic[:], big[:, 1, :, :, :].rearrange("p c b e -> p (c b) e"), AX, ALU.add)
            link(v.tensor_reduce(posc[:], big[:, 0, :, :, :].rearrange("p c b e -> p (c b) e"), AX, ALU.add))
            link(v.tensor_copy(posi[:], posc[:]))
            v.tensor_scalar(loi[:], posi[:], SLOTS - 1, None, ALU.bitwise_and)
            link(v.tensor_scalar(segi[:], posi[:], 6, None, ALU.arith_shift_right))
            v.tensor_tensor(hi[:], segi[:], hic[:], ALU.add)
            link(v.tensor_copy(posc[:], loi[:]))
            v.tensor_tensor(ohlo, spread(iota64[:], 1, 2 * TB), spread(posc[:], 2, 64), ALU.is_equal)
            link(v.tensor_tensor(ohhi, spread(iota64[:], 1, 2 * TB), spread(hi[:], 2, 64), ALU.is_equal))
            v.tensor_scalar(ohv[:, :, 0, :], ohhi, part1[:], None, ALU.mult)
            v.tensor_tensor(ohv[:, :, 1, :], ohhi, spread(blkcode[:], 2, 64), ALU.mult).then_inc(S["oh_ready"], 1)
            v.memset(gidx[:, MAXT:MAXT + RING + 1], BIG_ROW)
            dve.wait_ge(S["tab_mm"], 1)
            v.tensor_copy(dst[:], bank[4][:, MAXT:2 * MAXT])
            link(v.tensor_scalar(inv[:], bank[4][:, 0:MAXT], 0.0, float(BIG_ROW), ALU.is_equal, ALU.mult))
            link(v.scalar_tensor_tensor(dst[:], bank[4][:, 0:MAXT], -1.0, dst[:],
                                        ALU.add, ALU.add))
            link(v.tensor_scalar(dsti[:], dst[:], 0.0, None, ALU.max))
            link(v.tensor_scalar(toki[:], dsti[:], T - 1, None, ALU.bitwise_and))
            v.tensor_tensor(sidx[:], dsti[:], inv[:], ALU.add)
            v.tensor_tensor(gidx[:, 0:MAXT], toki[:], inv[:], ALU.add).then_inc(S["tab_ready"], 1)

            dve.wait_ge(S["exp_out"], 2)
            link(v.tensor_reduce(gs[:, 4, :], gw[:, 1, :, 0:NG], AX, ALU.add))
            link(v.tensor_scalar(gs[:, 5, :], gs[:, 8, :], 1.0, None, ALU.add))
            link(v.tensor_tensor(gs[:, 6, :], gs[:, 4, :], gs[:, 5, :], ALU.mult))
            link(v.reciprocal(wts[:, 0, :], gs[:, 6, :]))
            link(v.tensor_tensor(wts[:, 1, :], wts[:, 0, :], gs[:, 8, :], ALU.mult))

            def rows_T(t):
                dve.wait_ge(S["xg_mm"], 2 * t + 2)
                v.tensor_copy(xTs[:, 4:8, :].rearrange("p k n -> p (k n)"), bank[7][:]).then_inc(S["xtev_v"], 1)

            dve.wait_ge(S["tab_ready"], 2)
            tiles = dve.value_load(tab[0:1, PAIRS:PAIRS + 1], min_val=PAIRS, max_val=MAXT - 1)
            dve.wait_ge(S["rows_ready"], 1)
            v.tensor_copy(xg, ring[:, 0, :]).then_inc(S["xg_ready"], 1)
            rows_T(0)
            with dve.Fori(0, tiles) as t:
                dve.wait_ge(S["rows_ready"], t + 2)
                v.tensor_copy(xg, ring[:, (t + 1) % RING, :]).then_inc(S["xg_ready"], 1)
                dve.wait_ge(S["silu_g"], t + 1)
                dve.wait_ge(S["hidT_mm"], t + 1)
                v.tensor_tensor(hid, sil, bank[0][:, FF:2 * FF], ALU.mult).then_inc(S["hid_ready"], 1)
                rows_T(t + 1)
                dve.wait_ge(S["hidT_mm"], t + 2)
                v.tensor_copy(hidT[:, :, :].rearrange("p j n -> p (j n)"), bank[1][:, 0:2 * P])\
                    .then_inc(S["hidT_ev"], 1)
                dve.wait_ge(S["y_mm"], 2 * t + 1)
                dve.wait_ge(S["ys_free"], t + 1)
                v.tensor_copy(ys[:, t % RING, 0:BANK], bank[2][:]).then_inc(S["yev_v"], 1)
            for b in range(TB + 1):
                if b < TB:
                    dve.wait_ge(ld_y[b], 32)
                    for c in range(2):
                        if b and c:
                            mean_square(2, b - 1)
                        v.scalar_tensor_tensor(xr[:, b, :], yrow[:, 2 * ((b + 2) % TB) + c, :], wts[:, c, b:b + 1],
                                               xr[:, b, :], ALU.mult, ALU.add).then_inc(S["y_add"], 1)
                        dve.wait_ge(S["y_add"], 2 * b + c + 1)
                if b == TB:
                    mean_square(2, b - 1)
                if b:
                    dve.wait_ge(S["rstd_ready"], 2 * TB + b)
                    n = BANK if b < TB else D
                    v.scalar_tensor_tensor(xr[:, b - 1, 0:n], xr[:, b - 1, 0:n], rs[:, 2, b - 1:b], g_bc[:, 1, 0:n],
                                           ALU.mult, ALU.mult).then_inc(S["o_ready"], 1)


_INS = ["x", "g_mix", "w_in", "conv_w", "conv_b", "conv_ln_g", "conv_ln_b", "w_conv_out", "w_attn_out", "w_out",
        "rel_bias", "g_ffn", "w_group_router", "b_group_router", "w_expert_router", "b_expert_router",
        "w_e_gate", "w_e_up", "w_e_down", "g_final"]


def kernel(**inputs):
    import concourse.bacc as bacc
    from concourse.bass_utils import run_bass_kernel_spmd

    nc = bacc.Bacc("TRN2", target_bir_lowering=False, num_devices=1)
    arrays, args = {}, []
    for name in _INS:
        a = np.ascontiguousarray(inputs[name])
        arrays[f"in_{name}"] = a
        args.append(nc.dram_tensor(f"in_{name}", a.shape, mybir.dt.from_np(a.dtype), kind="ExternalInput").ap())
    shape = tuple(inputs["x"].shape)
    args.append(nc.dram_tensor("out_0", shape, F32, kind="ExternalOutput").ap())
    build(nc, *args)
    r = run_bass_kernel_spmd(nc, [arrays], core_ids=[0])
    return r.results[0]["out_0"]
```
